# Optimizing a Trainium2 kernel written in Bass

```python
import math
import jax, jax.numpy as jnp
from jax import lax
import numpy as np

D_MODEL = 2048
BATCH = 1
SEQ = 512
DEPTH = 1

N_META = 16
W_A = D_MODEL
H_A = 16
HD_A = W_A // H_A
CONV_A = 4
LRU_C = 8.0
W_B = D_MODEL
CONV_B = 31
EPS = 1e-6
SPLIT_SIZES = (W_A, W_A, W_B, W_B, W_B, D_MODEL, D_MODEL)
N_IN = sum(SPLIT_SIZES)
SPLIT_IDX = tuple(int(v) for v in np.cumsum(SPLIT_SIZES)[:-1])

kernel_name = "hybrid_rglru_conformer_conv_block"

def rms_norm(x, g):
    xf = x.astype(jnp.float32)
    y = xf * lax.rsqrt(jnp.mean(xf * xf, axis=-1, keepdims=True) + EPS)
    return (y * g.astype(jnp.float32)).astype(x.dtype)

def layer_norm(x, g, b):
    xf = x.astype(jnp.float32)
    mu = jnp.mean(xf, axis=-1, keepdims=True)
    xc = xf - mu
    var = jnp.mean(xc * xc, axis=-1, keepdims=True)
    y = xc * lax.rsqrt(var + EPS) * g.astype(jnp.float32) + b.astype(jnp.float32)
    return y.astype(x.dtype)

def causal_depthwise_conv(x, w, b):
    k, c = w.shape
    out = lax.conv_general_dilated(
        x, w[:, None, :].astype(x.dtype), window_strides=(1,), padding=[(k - 1, 0)],
        dimension_numbers=("NWC", "WIO", "NWC"), feature_group_count=c)
    return out + b.astype(x.dtype)

def rg_lru(x, w_r, b_r, w_i, b_i, lam):
    bsz, t, c = x.shape
    xh = x.reshape(bsz, t, H_A, HD_A)
    r = jax.nn.sigmoid(jnp.einsum("bthi,hij->bthj", xh, w_r).reshape(bsz, t, c) + b_r)
    i = jax.nn.sigmoid(jnp.einsum("bthi,hij->bthj", xh, w_i).reshape(bsz, t, c) + b_i)
    log_a = -LRU_C * r.astype(jnp.float32) * jax.nn.softplus(-lam.astype(jnp.float32))
    a = jnp.exp(log_a)
    mult = jnp.sqrt(jnp.maximum(-jnp.expm1(2.0 * log_a), 0.0))
    u = mult * (i * x).astype(jnp.float32)

    def combine(left, right):
        a1, b1 = left
        a2, b2 = right
        return a1 * a2, a2 * b1 + b2

    _, h = lax.associative_scan(combine, (a, u), axis=1)
    return h.astype(x.dtype)

def setup_inputs(seed: int = 0) -> dict:
    key = jax.random.key(seed)
    ks = jax.random.split(key, 24)
    f32 = jnp.float32
    nrm = lambda k, shape, s: (jax.random.normal(k, shape, f32) * s).astype(f32)
    x = jax.random.normal(ks[0], (BATCH, SEQ, D_MODEL), f32)
    meta = nrm(ks[1], (N_META, D_MODEL), 1.0)
    norm_g = 1.0 + nrm(ks[2], (DEPTH, D_MODEL), 0.05)
    w_in = nrm(ks[3], (DEPTH, D_MODEL, N_IN), D_MODEL ** -0.5)
    conv_a_w = nrm(ks[4], (DEPTH, CONV_A, W_A), CONV_A ** -0.5)
    conv_a_b = nrm(ks[5], (DEPTH, W_A), 0.02)
    w_rg = nrm(ks[6], (DEPTH, H_A, HD_A, HD_A), HD_A ** -0.5)
    b_rg = nrm(ks[7], (DEPTH, W_A), 0.02)
    w_ig = nrm(ks[8], (DEPTH, H_A, HD_A, HD_A), HD_A ** -0.5)
    b_ig = nrm(ks[9], (DEPTH, W_A), 0.02)
    a_c = jax.random.uniform(ks[10], (DEPTH, W_A), f32, 0.9, 0.999)
    s = a_c ** (1.0 / LRU_C)
    lru_lambda = jnp.log(s) - jnp.log1p(-s)
    conv_b_w = nrm(ks[11], (DEPTH, CONV_B, W_B), CONV_B ** -0.5)
    conv_b_b = nrm(ks[12], (DEPTH, W_B), 0.02)
    ln_b_g = 1.0 + nrm(ks[13], (DEPTH, W_B), 0.05)
    ln_b_b = nrm(ks[14], (DEPTH, W_B), 0.02)
    w_proj_a = nrm(ks[15], (DEPTH, W_A, D_MODEL), W_A ** -0.5)
    w_proj_b = nrm(ks[16], (DEPTH, W_B, D_MODEL), W_B ** -0.5)
    w_out = nrm(ks[17], (DEPTH, D_MODEL, D_MODEL), D_MODEL ** -0.5)
    final_g = 1.0 + nrm(ks[18], (D_MODEL,), 0.05)
    return {"x": x, "meta": meta, "norm_g": norm_g, "w_in": w_in,
            "conv_a_w": conv_a_w, "conv_a_b": conv_a_b, "w_rg": w_rg, "b_rg": b_rg,
            "w_ig": w_ig, "b_ig": b_ig, "lru_lambda": lru_lambda,
            "conv_b_w": conv_b_w, "conv_b_b": conv_b_b, "ln_b_g": ln_b_g, "ln_b_b": ln_b_b,
            "w_proj_a": w_proj_a, "w_proj_b": w_proj_b, "w_out": w_out, "final_g": final_g}

def reference(x, meta, norm_g, w_in, conv_a_w, conv_a_b, w_rg, b_rg, w_ig, b_ig, lru_lambda,
              conv_b_w, conv_b_b, ln_b_g, ln_b_b, w_proj_a, w_proj_b, w_out, final_g):
    bsz = x.shape[0]
    meta_b = jnp.broadcast_to(meta.astype(x.dtype)[None], (bsz, N_META, x.shape[-1]))
    h = jnp.concatenate([meta_b, x], axis=1)
    for l in range(DEPTH):
        hn = rms_norm(h, norm_g[l])
        z = jnp.einsum("btd,dn->btn", hn, w_in[l])
        xa, sa, vb, gb, sb, ma, mb = jnp.split(z, SPLIT_IDX, axis=-1)
        ya = causal_depthwise_conv(xa, conv_a_w[l], conv_a_b[l])
        ya = rg_lru(ya, w_rg[l], b_rg[l], w_ig[l], b_ig[l], lru_lambda[l])
        ya = ya * jax.nn.silu(sa)
        pa = jnp.einsum("btc,cd->btd", ya, w_proj_a[l])
        yb = vb * jax.nn.sigmoid(gb)
        yb = causal_depthwise_conv(yb, conv_b_w[l], conv_b_b[l])
        yb = jax.nn.silu(layer_norm(yb, ln_b_g[l], ln_b_b[l])) * jax.nn.silu(sb)
        pb = jnp.einsum("btc,cd->btd", yb, w_proj_b[l])
        merged = jax.nn.sigmoid(ma) * pa + jax.nn.sigmoid(mb) * pb
        h = h + jnp.einsum("btd,de->bte", merged, w_out[l])
    out = rms_norm(h, final_g)
    return out[:, N_META:, :]


_drawn_inputs = setup_inputs


def setup_inputs(seed=0):
    import zlib

    import numpy as np

    out = dict(_drawn_inputs(seed))
    spreads = {}
    factors = {'norm_g': 2.763,
     'b_rg': 32.829,
     'b_ig': 26.697,
     'conv_b_b': 8.0,
     'ln_b_g': 4.932,
     'ln_b_b': 8.0}
    for name, (base, spread) in spreads.items():
        noise = np.random.default_rng([zlib.crc32(name.encode()), seed]).standard_normal(out[name].shape)
        drawn = base * np.exp(spread * noise) if base else spread * noise
        out[name] = __import__('jax').numpy.asarray(drawn.astype(out[name].dtype))
    for name, factor in factors.items():
        out[name] = (out[name] * factor).astype(out[name].dtype)
    return out
```

```python
from contextlib import ExitStack

import concourse.bass as bass
from concourse import mybir

ALU = mybir.AluOpType
ACT = mybir.ActivationFunctionType
F32 = mybir.dt.float32
F32R = mybir.dt.float32r
ds = bass.ds

P = 128
EPS = 1e-6
LRU_C = 8.0
BODY = 16
RING = 2
NORM_G, CONV_A_B, B_R, B_I, LAMBDA, CONV_B_B, LN_G, LN_B = range(8)
CONV_A_W = 8
PER_BRANCH_BODY, PER_B_BODY = 80, 22
SERIES = 8


def plus(base, n):
    return base + n if n else base


def wait(engine, semaphore, value):
    if not (isinstance(value, int) and value <= 0):
        engine.wait_ge(semaphore, value)


class Steps:

    def __init__(self, engine, semaphore):
        self.engine, self.semaphore, self.base, self.n = engine, semaphore, 0, 0

    def __call__(self, instruction):
        instruction.then_inc(self.semaphore, 1)
        self.n += 1
        return plus(self.base, self.n)

    def done(self, value):
        self.engine.wait_ge(self.semaphore, value)

    def at(self, base):
        self.base, self.n = base, 0

    def total(self):
        assert isinstance(self.base, int)
        return self.base + self.n


def hybrid_trunk(nc, x, x_channels, meta_channels, parameters, w_in, w_rg, w_ig, w_proj_a, w_proj_b, w_out,
                 final_g, kernel_a, kernel_b, conv_spill, gated_a_spill, out):
    D = x.shape[2]
    SEQ = x.shape[1]
    META = meta_channels.shape[2]
    T = META + SEQ
    HALF = T // 2
    CT = D // P
    TT = SEQ // P
    KA, KB = kernel_a, kernel_b
    CONV_B_W = CONV_A_W + KA
    ROWS = CONV_B_W + KB
    DECAY, HALF_DECAY, COLS = ROWS, ROWS + 1, ROWS + 2
    PAIRS = CT // 2
    QUADS = CT // 4
    assert (CT, TT, w_in.shape[0]) == (16, 4, 1) and T % 4 == 0
    COL_XA, COL_SA, COL_VB, COL_GB, COL_SB, COL_MA, COL_MB = (n * D for n in range(7))

    w_in_v = w_in[0].rearrange("(k p) n -> p k n", p=P)
    w_pa_v = w_proj_a[0].rearrange("(k p) n -> p k n", p=P)
    w_pb_v = w_proj_b[0].rearrange("(k p) n -> p k n", p=P)
    w_out_v = w_out[0].rearrange("(k p) n -> p k n", p=P)
    x_v = x[0].rearrange("(t p) d -> t p d", p=P)
    out_v = out[0].rearrange("(t p) d -> t p d", p=P)

    ctx = ExitStack()
    with ctx:
        def sb(name, shape, dt=F32):
            return ctx.enter_context(nc.sbuf_tensor(name, shape, dt))

        def sem(name):
            return ctx.enter_context(nc.semaphore(name))

        x_hi, x_lo = sb("x_hi", [P, CT, T], F32R), sb("x_lo", [P, CT, T], F32R)
        y_hi, y_lo = sb("y_hi", [P, CT, SEQ], F32R), sb("y_lo", [P, CT, SEQ], F32R)
        raw = sb("raw", [P, RING, 1024])
        w_hi, w_lo = sb("w_hi", [P, RING, 1024], F32R), sb("w_lo", [P, RING, 1024], F32R)
        raw_v, w_hi_v, w_lo_v = (t[:, :, :].rearrange("p s (k n) -> p s k n", k=4) for t in (raw, w_hi, w_lo))
        region = sb("region", [P, CT * SEQ])
        tokens = region[:, :].rearrange("p (t d) -> p t d", t=TT)
        channels = region[:, :].rearrange("p (j s) -> p j s", j=CT)
        used = [0]

        def work(n, width):
            a = region[:, used[0]:used[0] + n * width].rearrange("p (n w) -> p n w", n=n)
            used[0] += n * width
            assert used[0] <= CT * SEQ
            return a

        xa_pad = work(2, 4 + T)
        rec = xa_pad[:, :, 4:]
        conv_a = work(2, T)
        inp = work(2, T)
        decay = work(2, T)
        sig_gb = work(2, T)
        yb_pad = work(2, KB - 1 + T)
        conv_b = work(2, SEQ)
        wide = sb("wide", [P, D])
        gate_raw = wide[:, 0:512].rearrange("p (g h j) -> p g h j", g=2, h=2)
        silu_sa = wide[:, 512:512 + 2 * SEQ].rearrange("p (t s) -> p t s", t=2)
        pairs = wide[:, :].rearrange("p (s t n) -> p s t n", s=2, t=2)
        meta_x, meta_squares = (wide[:, n * CT * META:(n + 1) * CT * META].rearrange("p (j m) -> p j m", j=CT)
                                for n in range(2))
        squares = wide[:, 512:].rearrange("p (n s) -> p n s", n=3)
        gate_hi, gate_lo = (sb(n, [P, 2, 2, P], F32R) for n in ("gate_hi", "gate_lo"))
        c_hi, c_lo = sb("c_hi", [P, HALF], F32R), sb("c_lo", [P, HALF], F32R)
        params = sb("params", [P, CT, COLS])
        lru_cols, conv_cols = sb("lru_cols", [P, 2, COLS]), sb("conv_cols", [P, 2, COLS])
        total = sb("total", [P, SEQ])
        average = sb("average", [P, P])
        stats = sb("stats", [P, 40])
        psum = ctx.enter_context(nc.psum_tensor("psum", [P, 8, 512], F32))

        sum_sq, rms, rstd = stats[:, 0:16], stats[:, 16:24], stats[:, 24:32]
        eps = stats[:, 32:33]

        params_loaded, meta_loaded = sem("params_loaded"), sem("meta_loaded")
        x_loaded = [sem(f"x_loaded{n}") for n in range(PAIRS)]
        x_reloaded = [sem(f"x_reloaded{t}") for t in range(TT)]
        average_ready, eps_ready = sem("average_ready"), sem("eps_ready")
        lambda_abs, lambda_exp = sem("lambda_abs"), sem("lambda_exp")
        x_squared, x_summed, x_means, x_rms = sem("x_squared"), sem("x_summed"), sem("x_means"), sem("x_rms")
        x_normed, norm_hi, norm_lo = sem("x_normed"), sem("norm_hi"), sem("norm_lo")
        raw_loaded = [sem(f"raw_loaded{s}") for s in range(RING)]
        hi_ready, lo_ready, multiplied = sem("hi_ready"), sem("lo_ready"), sem("multiplied")
        xa_copied, conv_a_done, c_hi_ready, c_lo_ready = (
            sem("xa_copied"), sem("conv_a_done"), sem("c_hi_ready"), sem("c_lo_ready"))
        gate_loaded, gate_hi_ready, gate_lo_ready = (
            sem("gate_loaded"), sem("gate_hi_ready"), sem("gate_lo_ready"))
        gates_multiplied, gates_read = sem("gates_multiplied"), sem("gates_read")
        sa_sigmoid, sa_silu, decay_ready, root_ready = (
            sem("sa_sigmoid"), sem("sa_silu"), sem("decay_ready"), sem("root_ready"))
        lru_out, gb_sigmoid, vb_gated = sem("lru_out"), sem("gb_sigmoid"), sem("vb_gated")
        conv_b_done, conv_b_spilled = sem("conv_b_done"), sem("conv_b_spilled")
        conv_b_loaded = [sem(f"conv_b_loaded{n}") for n in range(4)]
        summed, mean_ready, centred, squared = (
            sem("summed"), sem("mean_ready"), sem("centred"), sem("squared"))
        var_ready, std_ready = sem("var_ready"), sem("std_ready")
        ma_sigmoid, a_gated = sem("ma_sigmoid"), sem("a_gated")
        a_spilled = [sem(f"a_spilled{s}") for s in range(2)]
        a_loaded = [sem(f"a_loaded{s}") for s in range(2)]
        ln_affine, ln_sigmoid, sb_sigmoid, yb_ready, mb_sigmoid = (
            sem("ln_affine"), sem("ln_sigmoid"), sem("sb_sigmoid"), sem("yb_ready"), sem("mb_sigmoid"))
        merged_ready, g_loaded = sem("merged_ready"), sem("g_loaded")
        residual_added, out_squared, out_rms, out_rstd = (
            sem("residual_added"), sem("out_squared"), sem("out_rms"), sem("out_rstd"))
        out_ready, out_stored = sem("out_ready"), sem("out_stored")
        act_done, dve_done = sem("act_done"), sem("dve_done")

        B_A, B_N, B_B, B_O = PAIRS, PAIRS + QUADS, PAIRS + 2 * QUADS, PAIRS + 2 * QUADS + CT // 8
        END = B_O + D // 1024

        block = ctx.enter_context(nc.Block())

        @block.sync
        def _(sp):
            def body(b, sources):
                for p, source in enumerate(sources):
                    wait(sp, lo_ready, plus(b * BODY, p + 1 - RING))
                    width = source.shape[2]
                    to = raw[:, p % RING, :].rearrange("p (k n) -> p k n", n=width)
                    sp.dma_start(to, source).then_inc(raw_loaded[p % RING], 16)

            def columns(view, start):
                return [view[:, 4 * q:4 * q + 4, ds(start, 256)] for q in range(4)]

            def branch_body(i):
                body(i, [c for col in (COL_XA, COL_SA, COL_GB, COL_VB)
                         for c in columns(w_in_v, plus(i * 256, col))])

            for n in range(PAIRS):
                sp.dma_start(channels[:, 2 * n:2 * n + 2, :], x_channels[:, 2 * n:2 * n + 2, :])\
                    .then_inc(x_loaded[n], 16)
            branch_body(0)
            with sp.Fori(1, PAIRS) as i:
                branch_body(i)
            with sp.Fori(B_A, B_A + QUADS) as b:
                body(b, [c for s in range(2) for view, col in ((w_in_v, COL_MA), (w_pa_v, 0))
                         for c in columns(view, plus(b * 512, col + 256 * s - B_A * 512))])
            with sp.Fori(0, QUADS) as q:
                body(q + B_N, [c for s in range(2) for col in (COL_SB, COL_MB)
                               for c in columns(w_in_v, plus(q * 512, col + 256 * s))])
            with sp.Fori(0, CT // 8) as q:
                body(q + B_B, [c for s in range(4) for c in columns(w_pb_v, plus(q * 1024, 256 * s))])
            with sp.Fori(0, D // 1024) as q:
                body(q + B_O, [w_out_v[:, 2 * k:2 * k + 2, ds(plus(q * 1024, 512 * s), 512)]
                               for s in range(2) for k in range(8)])
            for t in range(TT):
                sp.wait_ge(out_ready, t + 1)
                sp.dma_start(out_v[t], tokens[:, t, :]).then_inc(out_stored, 16)
            sp.wait_ge(out_stored, 16 * TT)

        @block.gpsimd
        def _(pool):
            pool.memset(average[:, :], 1.0 / D).then_inc(average_ready, 1)

            def load_gates(i):
                wait(pool, gate_lo_ready, i)
                for g, w in enumerate((w_rg, w_ig)):
                    pool.dma_start(gate_raw[:, g], w[0, ds(2 * i, 2)].rearrange("h p j -> p h j"))\
                        .then_inc(gate_loaded, 16)

            def spill_conv(i):
                pool.wait_ge(conv_b_done, 2 * i)
                pool.dma_start(conv_spill[ds(2 * i - 2, 2)].rearrange("t p s -> p t s"), conv_b)\
                    .then_inc(conv_b_spilled, 16)

            def spill_a(q):
                for s in range(2):
                    pool.wait_ge(a_gated, plus(4 * q, 2 * s + 2))
                    pool.dma_start(gated_a_spill[ds(plus(4 * q, 2 * s), 2)].rearrange("t p s -> p t s"),
                                   pairs[:, s]).then_inc(a_spilled[s], 16)

            pool.wait_ge(norm_lo, 1)
            load_gates(0)
            with pool.Fori(1, PAIRS) as i:
                load_gates(i)
                spill_conv(i)
            spill_conv(PAIRS)
            spill_a(0)
            pool.wait_ge(conv_b_spilled, 16 * PAIRS)
            pool.wait_ge(mean_ready, 1)
            for n in range(4):
                pool.dma_start(channels[:, 4 * n:4 * n + 4], conv_spill[4 * n:4 * n + 4].rearrange("t p s -> p t s"))\
                    .then_inc(conv_b_loaded[n], 16)
            with pool.Fori(1, QUADS) as q:
                spill_a(q)

            def load_a(q, s):
                wait(pool, merged_ready, plus(8 * q, 2 * s - 2))
                pool.dma_start(pairs[:, s % 2], gated_a_spill[ds(plus(8 * q, 2 * s), 2)].rearrange("t p s -> p t s"))\
                    .then_inc(a_loaded[s % 2], 16)

            for s in range(2):
                pool.wait_ge(a_spilled[s], 16 * PAIRS // 2)
            pool.wait_ge(yb_ready, CT)
            for s in range(4):
                load_a(0, s)
            with pool.Fori(1, CT // 8) as q:
                for s in range(4):
                    load_a(q, s)
            pool.wait_ge(merged_ready, CT)
            for t in range(TT):
                pool.wait_ge(multiplied, B_O * BODY + t + 1)
                pool.dma_start(tokens[:, t, :], x_v[t]).then_inc(x_reloaded[t], 16)
            pool.dma_start(wide[:, :], final_g.rearrange("(a d) -> a d", a=1).broadcast_to([P, D])).then_inc(g_loaded, 16)

        @block.tensor
        def _(pe):
            def multiply(b, p, banks, width, first_token, operand, group):
                n = plus(b * BODY, p)
                hi, lo = operand

                def passes(weights, parts):
                    for k in range(4):
                        for m in range(2):
                            for part in parts:
                                for piece, bank in enumerate(banks[m]):
                                    t0 = first_token + piece * width
                                    last = pe.matmul(
                                        psum[:, bank, 0:width], weights[:, p % RING, k, m * P:(m + 1) * P],
                                        part[:, 4 * group + k, t0:t0 + width],
                                        start=group == 0 and k == 0 and weights is w_hi_v and part is hi,
                                        stop=group == 3 and k == 3 and weights is w_lo_v)
                    return last

                pe.wait_ge(hi_ready, plus(n, 1))
                passes(w_hi_v, (hi, lo))
                pe.wait_ge(lo_ready, plus(n, 1))
                passes(w_lo_v, (hi,)).then_inc(multiplied, 1)

            def gate_round(i, n):
                pe.wait_ge(c_hi_ready, plus(4 * i, n + 1))
                pe.wait_ge(c_lo_ready, plus(4 * i, n + 1))
                wait(pe, gates_read, plus(4 * i, n))
                for g in range(2):
                    for weights, part in ((gate_hi, c_hi), (gate_hi, c_lo), (gate_lo, c_hi)):
                        last = pe.matmul(psum[:, 6 + g, 0:HALF], weights[:, g, n // 2, :], part[:, :],
                                         start=weights is gate_hi and part is c_hi, stop=weights is gate_lo)
                last.then_inc(gates_multiplied, 1)

            x_all, x_seq, y_all = (x_hi, x_lo), (x_hi, x_lo), (y_hi, y_lo)

            def branch_body(i):
                wait(pe, gb_sigmoid, 2 * i)
                for g in range(4):
                    if isinstance(i, int):
                        pe.wait_ge(norm_lo, 4 * g + 5)
                    multiply(i, g, ((0, 1), (2, 3)), HALF, 0, x_all, g)
                wait(pe, vb_gated, 2 * i)
                for g in range(4):
                    multiply(i, 4 + g, ((4,), (5,)), SEQ, META, x_seq, g)
                pe.wait_ge(gate_hi_ready, plus(i, 1))
                pe.wait_ge(gate_lo_ready, plus(i, 1))
                pe.wait_ge(xa_copied, plus(2 * i, 2))
                for g in range(4):
                    gate_round(i, g)
                    multiply(i, 8 + g, ((0, 1), (2, 3)), HALF, 0, x_all, g)
                pe.wait_ge(sa_silu, plus(2 * i, 2))
                pe.wait_ge(gates_read, plus(4 * i, 4))
                for g in range(4):
                    multiply(i, 12 + g, ((4, 5), (6, 7)), HALF, 0, x_all, g)

            def a_body(q, mean=False):
                for s in range(2):
                    wait(pe, ma_sigmoid, plus(4 * q, 2 * s))
                    for g in range(4):
                        multiply(plus(q, B_A), 8 * s + g, ((0,), (1,)), SEQ, META, x_seq, g)
                        if mean and s == 0 and g == 3:
                            pe.wait_ge(summed, CT)
                            pe.wait_ge(average_ready, 1)
                            pe.matmul(psum[:, 7, :], average[:, :], total[:, :], start=True, stop=True)\
                                .then_inc(mean_ready, 1)
                    if isinstance(q, int) and (q, s) == (0, 0):
                        pe.wait_ge(lru_out, CT)
                    wait(pe, a_gated, plus(4 * q, 2 * s))
                    for g in range(4):
                        multiply(plus(q, B_A), 8 * s + 4 + g, ((2,), (3,)), SEQ, 0, y_all, g)

            def b_body(q):
                for s in range(2):
                    wait(pe, yb_ready, plus(4 * q, 2 * s))
                    for g in range(4):
                        multiply(plus(q, B_N), 8 * s + g, ((0,), (1,)), SEQ, META, x_seq, g)
                    if isinstance(q, int) and (q, s) == (0, 0):
                        pe.wait_ge(a_gated, CT)
                    wait(pe, mb_sigmoid, plus(2 * q, s))
                    for g in range(4):
                        multiply(plus(q, B_N), 8 * s + 4 + g, ((2,), (3,)), SEQ, META, x_seq, g)

            pe.wait_ge(average_ready, 1)
            pe.wait_ge(x_summed, 1 + CT)
            pe.matmul(psum[:, 6, 0:META], average[:, :], stats[:, 0:META], start=True, stop=True)
            pe.matmul(psum[:, 7, :], average[:, :], total[:, :], start=True, stop=True).then_inc(x_means, 1)
            branch_body(0)
            with pe.Fori(1, PAIRS) as i:
                branch_body(i)
            pe.wait_ge(gb_sigmoid, 2 * PAIRS)
            a_body(0)
            a_body(1, mean=True)
            with pe.Fori(2, QUADS) as q:
                a_body(q)
            pe.wait_ge(summed, 2 * CT)
            pe.matmul(psum[:, 6, :], average[:, :], total[:, :], start=True, stop=True).then_inc(var_ready, 1)
            b_body(0)
            with pe.Fori(1, QUADS) as q:
                b_body(q)

            for q in range(CT // 8):
                for s in range(4):
                    wait(pe, merged_ready, 8 * q + 2 * s - 6)
                    if (q, s) == (0, 1):
                        pe.wait_ge(mb_sigmoid, PAIRS)
                    for g in range(4):
                        if (q, s) == (0, 0):
                            pe.wait_ge(yb_ready, 4 * g + 4)
                        multiply(B_B + q, 4 * s + g, ((2 * s,), (2 * s + 1,)), SEQ, 0, y_all, g)

            for n in range(D // 512):
                banks = 4 * (n % 2)
                wait(pe, out_squared, 4 * n - 4)
                for g in range(8):
                    if n == 0:
                        pe.wait_ge(merged_ready, max(2 * g + 2, CT - 4))
                    hi, lo = (w[:, g % RING, :].rearrange("p (k n) -> p k n", k=2) for w in (w_hi, w_lo))
                    for ready, weights, parts in ((hi_ready, hi, (x_hi, x_lo)), (lo_ready, lo, (x_hi,))):
                        pe.wait_ge(ready, B_O * BODY + 8 * n + g + 1)
                        for t in range(TT):
                            for k in range(2):
                                for part in parts:
                                    last = pe.matmul(
                                        psum[:, banks + t, :], part[:, 2 * g + k, META + t * P:META + (t + 1) * P],
                                        weights[:, k, :],
                                        start=g == 0 and k == 0 and part is x_hi and weights is hi,
                                        stop=g == 7 and k == 1 and weights is lo)
                    last.then_inc(multiplied, 1)

        @block.scalar
        def _(act):
            steps = Steps(act, act_done)

            def cut_hi(b, p):
                n = plus(b * BODY, p)
                act.wait_ge(raw_loaded[p % RING], plus(b * (16 * BODY // RING), 16 * (p // RING + 1)))
                wait(act, multiplied, plus(n, 1 - RING))
                act.activation(w_hi[:, p % RING, :], raw[:, p % RING, :], ACT.Copy).then_inc(hi_ready, 1)

            def group_done(b, chunks):
                act.wait_ge(multiplied, plus(b * BODY, chunks))

            def read_gates(i, n):
                t, tok = n // 2, slice((n % 2) * HALF, (n % 2 + 1) * HALF)
                act.wait_ge(gates_multiplied, plus(4 * i, n + 1))
                act.activation(rec[:, t, tok], psum[:, 6, 0:HALF], ACT.Sigmoid, bias=lru_cols[:, t, B_R:B_R + 1])
                act.activation(inp[:, t, tok], psum[:, 7, 0:HALF], ACT.Sigmoid, bias=lru_cols[:, t, B_I:B_I + 1])\
                    .then_inc(gates_read, 1)

            def cut_c_hi(i, n):
                t, tok = n // 2, slice((n % 2) * HALF, (n % 2 + 1) * HALF)
                act.wait_ge(conv_a_done, plus(2 * i, t + 1))
                wait(act, gates_multiplied, plus(4 * i, n))
                act.activation(c_hi[:, :], conv_a[:, t, tok], ACT.Copy).then_inc(c_hi_ready, 1)

            def branch_body(i):
                first = isinstance(i, int)
                for p in range(BODY):
                    cut_hi(i, p)
                    if first and p == 1:
                        act.wait_ge(x_normed, 1)
                        act.activation(x_hi[:, :, 0:META], meta_x, ACT.Copy).then_inc(norm_hi, 1)
                    if first and 1 <= p < 4:
                        for j in range(4 * p if p > 1 else 0, 4 * p + 4):
                            act.wait_ge(x_normed, j + 2)
                            act.activation(x_hi[:, j, META:T], channels[:, j, :], ACT.Copy).then_inc(norm_hi, 1)
                    if first and p == 4:
                        act.wait_ge(lambda_abs, 1)
                        act.activation(stats[:, 0:CT], stats[:, 0:CT], ACT.Exp, scale=-1.0).then_inc(lambda_exp, 1)
                    if p == 3:
                        act.wait_ge(gate_loaded, plus(32 * i, 32))
                        wait(act, gates_multiplied, 4 * i)
                        act.activation(gate_hi[:, :, :, :], gate_raw, ACT.Copy).then_inc(gate_hi_ready, 1)
                    if p == 5:
                        group_done(i, 4)
                        wait(act, lru_out, 2 * i)
                        if first:
                            act.wait_ge(norm_lo, 1 + CT)
                        for t in range(2):
                            act.activation(xa_pad[:, t, 4:].rearrange("p (h n) -> p h n", h=2),
                                           psum[:, 2 * t:2 * t + 2, 0:HALF], ACT.Copy).then_inc(xa_copied, 1)
                    if 8 <= p < 12:
                        cut_c_hi(i, p - 8)
                    if p == 9:
                        group_done(i, 8)
                        for t in range(2):
                            act.activation(silu_sa[:, t, :], psum[:, 4 + t, :], ACT.Sigmoid).then_inc(sa_sigmoid, 1)
                    if 9 <= p < 13:
                        read_gates(i, p - 9)
                    if p == 12:
                        act.wait_ge(gates_read, plus(4 * i, 4))
                        for t in range(2):
                            act.activation(decay[:, t, :], rec[:, t, :], ACT.Exp,
                                           scale=lru_cols[:, t, DECAY:DECAY + 1]).then_inc(decay_ready, 1)
                        for t in range(2):
                            v = steps(act.activation(rec[:, t, :], rec[:, t, :], ACT.Tanh,
                                                     scale=lru_cols[:, t, HALF_DECAY:HALF_DECAY + 1]))
                    if p == 13:
                        steps.done(v)
                        for t in range(2):
                            act.activation(rec[:, t, :], rec[:, t, :], ACT.Sqrt).then_inc(root_ready, 1)
                    if p == 14:
                        group_done(i, 12)
                        for t in range(2):
                            act.activation(sig_gb[:, t, :].rearrange("p (h n) -> p h n", h=2),
                                           psum[:, 2 * t:2 * t + 2, 0:HALF], ACT.Sigmoid).then_inc(gb_sigmoid, 1)

            def a_body(q, squares=False):
                b = plus(q, B_A)
                for p in range(BODY):
                    cut_hi(b, p)
                    if p in (5, 13):
                        s = p // 8
                        group_done(b, 8 * s + 4)
                        wait(act, a_spilled[s], 16 * q)
                        if isinstance(q, int) and q == 0:
                            act.wait_ge(lru_out, CT)
                        for t in range(2):
                            act.activation(pairs[:, s, t, :], psum[:, t, :], ACT.Sigmoid).then_inc(ma_sigmoid, 1)
                    if squares and 2 <= p < 10:
                        u = p - 2
                        act.wait_ge(centred, plus(8 * q, u + 1 - 16))
                        act.wait_ge(summed, plus(8 * q, u - 1))
                        act.activation(psum[:, 4 + u % 2, :], channels[:, ds(plus(8 * q, u - 16), 1), :].rearrange("p a s -> p (a s)"),
                                       ACT.Square).then_inc(squared, 1)

            def read_mb(j):
                act.wait_ge(yb_ready, plus(2 * j, 2))
                act.activation(channels[:, ds(2 * j, 2), :], psum[:, 2:4, :], ACT.Sigmoid).then_inc(mb_sigmoid, 1)

            def b_body(q, first=False):
                b = plus(q, B_N)
                for p in range(BODY):
                    cut_hi(b, p)
                    if first and p == 0:
                        act.wait_ge(var_ready, 1)
                        act.activation(psum[:, 6, :], psum[:, 6, :], ACT.Sqrt, bias=eps).then_inc(std_ready, 1)
                    if p in (1, 9) and not (first and p == 1):
                        group_done(b, p - 1)
                        read_mb(plus(2 * q, p // 8 - 1))
                    if p in (2, 3, 10, 11):
                        s, t = p // 8, p % 2
                        j = plus(4 * q, 2 * s + t)
                        act.wait_ge(ln_affine, plus(j, 1))
                        act.activation(psum[:, 4 + t, :], channels[:, ds(j, 1), :].rearrange("p a s -> p (a s)"),
                                       ACT.Sigmoid).then_inc(ln_sigmoid, 1)
                    if p in (5, 13):
                        s = p // 8
                        group_done(b, 8 * s + 4)
                        if first and s == 0:
                            for n in range(2):
                                act.wait_ge(a_spilled[n], 16 * QUADS)
                        wait(act, yb_ready, plus(4 * q, 2 * s))
                        for t in range(2):
                            act.activation(pairs[:, 0, t, :], psum[:, t, :], ACT.Sigmoid).then_inc(sb_sigmoid, 1)

            act.dma_start(params[:, :, :], parameters).then_inc(params_loaded, 16)
            act.dma_start(meta_x, meta_channels).then_inc(meta_loaded, 16)
            act.wait_ge(eps_ready, 1)
            act.activation(stats[:, 33:34], eps, ACT.Sqrt)
            act.wait_ge(meta_loaded, 16)
            act.activation(meta_squares, meta_x, ACT.Square).then_inc(x_squared, 1)
            for j in range(CT):
                act.wait_ge(x_loaded[j // 2], 16)
                wait(act, x_summed, j - 1 if j > 2 else 0)
                act.activation(squares[:, j % 3, :], channels[:, j, :], ACT.Square).then_inc(x_squared, 1)
            act.wait_ge(x_means, 1)
            act.activation(psum[:, 6, 0:META], psum[:, 6, 0:META], ACT.Sqrt, bias=eps)
            act.activation(psum[:, 7, :], psum[:, 7, :], ACT.Sqrt, bias=eps).then_inc(x_rms, 1)

            branch_body(0)
            with act.Fori(1, PAIRS) as i:
                steps.at(2 * i)
                branch_body(i)
            a_body(0)
            a_body(1)
            with act.Fori(2, QUADS) as q:
                a_body(q, squares=True)
            b_body(0, first=True)
            with act.Fori(1, QUADS) as q:
                b_body(q)
            for p in range(2):
                cut_hi(B_B, p)
            group_done(B_B, 0)
            read_mb(PAIRS - 1)
            for p in range(2, BODY):
                cut_hi(B_B, p)
            for p in range(BODY):
                cut_hi(B_B + 1, p)

            def square_rows(n):
                for t in range(TT):
                    act.wait_ge(residual_added, 4 * n + t + 1)
                    act.activation(psum[:, 4 * (n % 2) + t, :], tokens[:, t, n * 512:(n + 1) * 512], ACT.Square,
                                   accum_out=sum_sq[:, 4 * t + n:4 * t + n + 1]).then_inc(out_squared, 1)

            for n in range(D // 512):
                for p in range(8):
                    cut_hi(B_O + n // 2, 8 * (n % 2) + p)
                    if n > 0 and p == 3:
                        square_rows(n - 1)
            square_rows(D // 512 - 1)
            for t in range(TT):
                act.wait_ge(out_rms, t + 1)
                act.activation(rms[:, t:t + 1], rms[:, t:t + 1], ACT.Sqrt, scale=1.0 / D, bias=eps).then_inc(out_rstd, 1)

        @block.vector
        def _(dve):
            steps = Steps(dve, dve_done)

            def cut_lo(b, p):
                dve.wait_ge(hi_ready, plus(b * BODY, p + 1))
                dve.tensor_tensor(w_lo[:, p % RING, :], raw[:, p % RING, :], w_hi[:, p % RING, :].bitcast(F32),
                                  ALU.subtract).then_inc(lo_ready, 1)

            def group_done(b, chunks):
                dve.wait_ge(multiplied, plus(b * BODY, chunks))

            def cut(values, done, hi, lo, j, tokens_of, ready):
                parts = [[part[:, ds(plus(j, t), 1), tokens_of].rearrange("p a s -> p (a s)") for t in range(2)]
                         for part in (hi, lo)]
                for t in range(2):
                    steps.done(done[t])
                    done[t] = steps(dve.tensor_copy(parts[0][t], values[t]))
                for t in range(2):
                    steps.done(done[t])
                    dve.tensor_tensor(parts[1][t], values[t], parts[0][t].bitcast(F32), ALU.subtract).then_inc(ready, 1)

            TAPS = [0, 3, 3, 3, 3, 1, 1, 3, 2, 3, 2, 3, 3, 1, 0, 0]
            assert sum(TAPS) == KB

            def conv_b_taps(i, p, before):
                for k in range(sum(TAPS[:p]), sum(TAPS[:p + 1])):
                    for t in range(2):
                        moved = yb_pad[:, t, META + k:META + k + SEQ]
                        w = conv_cols[:, t, CONV_B_W + k:CONV_B_W + k + 1]
                        if k == 0:
                            wait(dve, conv_b_spilled, 16 * (i - 1))
                            dve.wait_ge(vb_gated, plus(2 * i, t - 1))
                            ins = dve.tensor_scalar(conv_b[:, t, :], moved, w, conv_cols[:, t, CONV_B_B:CONV_B_B + 1],
                                                    ALU.mult, ALU.add)
                        else:
                            steps.done(before[t])
                            ins = dve.scalar_tensor_tensor(conv_b[:, t, :], moved, w, conv_b[:, t, :], ALU.mult, ALU.add)
                        if k == KB - 1:
                            ins.then_inc(conv_b_done, 1)
                        else:
                            before[t] = steps(ins)

            def add_total(i):
                for t in range(2):
                    dve.wait_ge(conv_b_done, plus(2 * i, t - 1))
                    wait(dve, summed, plus(2 * i, t - 2))
                    dve.tensor_tensor(total[:, :], total[:, :], conv_b[:, t, :], ALU.add).then_inc(summed, 1)

            def branch_body(i, first=False):
                taps = [None, None]
                conv = [None, None]
                for p in range(BODY):
                    if first and p < 4:
                        norm_tiles(p)
                    else:
                        cut_lo(i, p)
                    if first and p == 3:
                        steps(dve.memset(xa_pad[:, :, 0:4], 0.0))
                        one_step(dve.memset(yb_pad[:, :, 0:KB - 1], 0.0))
                        absolute_lambda()
                    if first and p == 4:
                        decay_columns()
                    if p == (4 if first else 0):
                        if not first:
                            c = steps(dve.tensor_copy(conv_cols[:, :, :], lru_cols[:, :, :]))
                            steps.done(c)
                        wait(dve, root_ready, 2 * i)
                        c = steps(dve.tensor_copy(lru_cols[:, :, :], params[:, ds(2 * i, 2), :]))
                        steps.done(c)
                    if p == 4:
                        dve.wait_ge(gate_hi_ready, plus(i, 1))
                        dve.tensor_tensor(gate_lo[:, :, :, :], gate_raw, gate_hi[:, :, :, :].bitcast(F32), ALU.subtract)\
                            .then_inc(gate_lo_ready, 1)
                    if p in (5, 6):
                        for k in range(2 * (p - 5), 2 * (p - 5) + 2):
                            for t in range(2):
                                moved = xa_pad[:, t, 4 - (KA - 1) + k:4 - (KA - 1) + k + T]
                                w = lru_cols[:, t, CONV_A_W + k:CONV_A_W + k + 1]
                                if k == 0:
                                    dve.wait_ge(xa_copied, plus(2 * i, t + 1))
                                    conv[t] = steps(dve.tensor_scalar(
                                        conv_a[:, t, :], moved, w, lru_cols[:, t, CONV_A_B:CONV_A_B + 1], ALU.mult, ALU.add))
                                else:
                                    steps.done(conv[t])
                                    ins = dve.scalar_tensor_tensor(conv_a[:, t, :], moved, w, conv_a[:, t, :],
                                                                   ALU.mult, ALU.add)
                                    if k == KA - 1:
                                        ins.then_inc(conv_a_done, 1)
                                    else:
                                        conv[t] = steps(ins)
                    if 8 <= p < 12:
                        n = p - 8
                        t, tok = n // 2, slice((n % 2) * HALF, (n % 2 + 1) * HALF)
                        dve.wait_ge(c_hi_ready, plus(4 * i, n + 1))
                        dve.tensor_tensor(c_lo[:, :], conv_a[:, t, tok], c_hi[:, :].bitcast(F32), ALU.subtract)\
                            .then_inc(c_lo_ready, 1)
                    if p == 10:
                        for t in range(2):
                            dve.wait_ge(sa_sigmoid, plus(2 * i, t + 1))
                            dve.tensor_tensor(silu_sa[:, t, :], silu_sa[:, t, :], psum[:, 4 + t, :], ALU.mult)\
                                .then_inc(sa_silu, 1)
                    if p == 13:
                        dve.wait_ge(gates_read, plus(4 * i, 4))
                        gated = [steps(dve.tensor_tensor(inp[:, t, :], inp[:, t, :], conv_a[:, t, :], ALU.mult))
                                 for t in range(2)]
                    if p == 14:
                        factor = []
                        for t in range(2):
                            dve.wait_ge(root_ready, plus(2 * i, t + 1))
                            steps.done(gated[t])
                            factor.append(steps(dve.scalar_tensor_tensor(
                                conv_a[:, t, :], decay[:, t, :], 1.0, rec[:, t, :], ALU.add, ALU.mult)))
                        for t in range(2):
                            steps.done(factor[t])
                            factor[t] = steps(dve.tensor_tensor(inp[:, t, :], inp[:, t, :], conv_a[:, t, :], ALU.mult))
                    if p == 15:
                        state, gate = [], []
                        for t in range(2):
                            steps.done(factor[t])
                            state.append(steps(dve.tensor_tensor_scan(
                                rec[:, t, :], decay[:, t, :], inp[:, t, :], 0.0, ALU.mult, ALU.add)))
                        for t in range(2):
                            steps.done(state[t])
                            dve.wait_ge(sa_silu, plus(2 * i, t + 1))
                            gate.append(steps(dve.tensor_tensor(
                                silu_sa[:, t, :], rec[:, t, META:T], silu_sa[:, t, :], ALU.mult)))
                        cut([silu_sa[:, t, :] for t in range(2)], gate, y_hi, y_lo, 2 * i, slice(0, SEQ), lru_out)
                    if not first:
                        conv_b_taps(i, p, taps)
                        if p == 14:
                            add_total(i)
                gate_vb(i)

            def gate_vb(i):
                group_done(i, 16)
                for t in range(2):
                    dve.wait_ge(gb_sigmoid, plus(2 * i, t + 1))
                    dve.tensor_tensor(yb_pad[:, t, KB - 1:].rearrange("p (h n) -> p h n", h=2),
                                      sig_gb[:, t, :].rearrange("p (h n) -> p h n", h=2),
                                      psum[:, 4 + 2 * t:6 + 2 * t, 0:HALF], ALU.mult).then_inc(vb_gated, 1)

            def channel(j):
                return channels[:, ds(j, 1), :].rearrange("p a s -> p (a s)")

            def a_body(q, conv=False, moments=False):
                b = plus(q, B_A)
                taps = [None, None]
                for p in range(BODY):
                    cut_lo(b, p)
                    if conv:
                        if p == 0:
                            c = steps(dve.tensor_copy(conv_cols[:, :, :], lru_cols[:, :, :]))
                            steps.done(c)
                        conv_b_taps(PAIRS, p, taps)
                        if p == 14:
                            add_total(PAIRS)
                    if p == 9:
                        gate_pa(q, b, 0)
                    if moments and 1 <= p < 9:
                        u = p - 1
                        j = plus(8 * q, u - 16)
                        dve.tensor_tensor(channel(j), channel(j), psum[:, 7, :], ALU.subtract).then_inc(centred, 1)
                    if moments and 3 <= p < 11:
                        u = p - 3
                        dve.wait_ge(squared, plus(8 * q, u + 1 - 16))
                        dve.wait_ge(summed, plus(8 * q, u))
                        dve.tensor_tensor(total[:, :], total[:, :], psum[:, 4 + u % 2, :], ALU.add).then_inc(summed, 1)
                gate_pa(q, b, 1)

            def gate_pa(q, b, s):
                group_done(b, 8 * s + 8)
                for t in range(2):
                    dve.wait_ge(ma_sigmoid, plus(4 * q, 2 * s + t + 1))
                    dve.tensor_tensor(pairs[:, s, t, :], pairs[:, s, t, :], psum[:, 2 + t, :], ALU.mult)\
                        .then_inc(a_gated, 1)

            def b_body(q, first=False):
                b = plus(q, B_N)
                for p in range(BODY):
                    cut_lo(b, p)
                    if first and p == 1:
                        dve.wait_ge(std_ready, 1)
                        one_step(dve.reciprocal(psum[:, 7, :], psum[:, 6, :]))
                    s, t = p // 8, p % 2
                    if p in (0, 8):
                        c = steps(dve.tensor_copy(lru_cols[:, :, :], params[:, ds(plus(4 * q, 2 * s), 2), :]))
                        steps.done(c)
                    if p in (1, 9):
                        scaled_v = [steps(dve.tensor_tensor(channel(plus(4 * q, 2 * s + t)), channel(plus(4 * q, 2 * s + t)),
                                                            psum[:, 7, :], ALU.mult)) for t in range(2)]
                        for t in range(2):
                            steps.done(scaled_v[t])
                            c = channel(plus(4 * q, 2 * s + t))
                            dve.tensor_scalar(c, c, lru_cols[:, t, LN_G:LN_G + 1], lru_cols[:, t, LN_B:LN_B + 1],
                                              ALU.mult, ALU.add).then_inc(ln_affine, 1)
                    if p in (4, 12):
                        silu = []
                        for t in range(2):
                            j = plus(4 * q, 2 * s + t)
                            dve.wait_ge(ln_sigmoid, plus(j, 1))
                            silu.append(steps(dve.tensor_tensor(channel(j), channel(j), psum[:, 4 + t, :], ALU.mult)))
                    if p in (6, 14):
                        v = []
                        for t in range(2):
                            dve.wait_ge(sb_sigmoid, plus(4 * q, 2 * s + t + 1))
                            v.append(steps(dve.tensor_tensor(pairs[:, 0, t, :], pairs[:, 0, t, :], psum[:, t, :], ALU.mult)))
                        for t in range(2):
                            j = plus(4 * q, 2 * s + t)
                            steps.done(v[t])
                            v[t] = steps(dve.tensor_tensor(pairs[:, 0, t, :], pairs[:, 0, t, :], channel(j), ALU.mult))
                        cut([pairs[:, 0, t, :] for t in range(2)], v, y_hi, y_lo, plus(4 * q, 2 * s), slice(0, SEQ),
                            yb_ready)

            def merge(q, s):
                group_done(plus(q, B_B), 4 * s + 4)
                dve.wait_ge(mb_sigmoid, plus(4 * q, s + 1))
                v = [steps(dve.tensor_tensor(channel(plus(8 * q, 2 * s + t)), channel(plus(8 * q, 2 * s + t)),
                                             psum[:, 2 * s + t, :], ALU.mult)) for t in range(2)]
                dve.wait_ge(a_loaded[s % 2], plus(32 * q, 16 * (s // 2 + 1)))
                for t in range(2):
                    j = plus(8 * q, 2 * s + t)
                    steps.done(v[t])
                    v[t] = steps(dve.tensor_tensor(channel(j), channel(j), pairs[:, s % 2, t, :], ALU.add))
                cut([channel(plus(8 * q, 2 * s + t)) for t in range(2)], v, x_hi, x_lo, plus(8 * q, 2 * s),
                    slice(META, T), merged_ready)

            def add_residual(n):
                group_done(B_O, 8 * n + 8)
                for t in range(TT):
                    rows = tokens[:, t, n * 512:(n + 1) * 512]
                    dve.wait_ge(x_reloaded[t], 16)
                    dve.tensor_tensor(rows, rows, psum[:, 4 * (n % 2) + t, :], ALU.add).then_inc(residual_added, 1)

            def one_step(ins):
                steps.done(steps(ins))

            def tile_lo(j):
                dve.wait_ge(norm_hi, 2 + j)
                dve.tensor_tensor(x_lo[:, j, META:T], channels[:, j, :], x_hi[:, j, META:T].bitcast(F32),
                                  ALU.subtract).then_inc(norm_lo, 1)

            def norm_tiles(p):
                for j in range(4 * p, 4 * p + 4):
                    dve.scalar_tensor_tensor(channels[:, j, :], channels[:, j, :], params[:, j, NORM_G:NORM_G + 1],
                                             psum[:, 7, :], ALU.mult, ALU.mult).then_inc(x_normed, 1)
                    if j > 4 * p:
                        tile_lo(j - 1)
                cut_lo(0, p)
                tile_lo(4 * p + 3)

            lam = params[:, :, LAMBDA:LAMBDA + 1].rearrange("p j c -> p (j c)")
            soft = params[:, :, DECAY:DECAY + 1].rearrange("p j c -> p (j c)")
            half_soft = params[:, :, HALF_DECAY:HALF_DECAY + 1].rearrange("p j c -> p (j c)")
            z, s, s2 = stats[:, 0:CT], stats[:, CT:2 * CT], total[:, 0:CT]
            series = total[:, CT:2 * CT]

            def absolute_lambda():
                one_step(dve.tensor_scalar(s, lam, -1.0, None, ALU.mult))
                dve.tensor_tensor(z, lam, s, ALU.max).then_inc(lambda_abs, 1)
                one_step(dve.tensor_scalar(soft, s, 0.0, None, ALU.max))

            def decay_columns():
                dve.wait_ge(lambda_exp, 1)
                one_step(dve.tensor_scalar(s, z, 2.0, None, ALU.add))
                one_step(dve.reciprocal(s, s))
                one_step(dve.tensor_tensor(s, s, z, ALU.mult))
                one_step(dve.tensor_tensor(s2, s, s, ALU.mult))
                one_step(dve.tensor_scalar(series, s2, 1.0 / (2 * SERIES - 1), None, ALU.mult))
                for n in range(SERIES - 2, 0, -1):
                    one_step(dve.scalar_tensor_tensor(series, series, 1.0 / (2 * n + 1), s2, ALU.add, ALU.mult))
                one_step(dve.scalar_tensor_tensor(series, series, 1.0, s, ALU.add, ALU.mult))
                one_step(dve.scalar_tensor_tensor(soft, series, 2.0, soft, ALU.mult, ALU.add))
                one_step(dve.tensor_scalar(half_soft, soft, LRU_C / 2, None, ALU.mult))
                one_step(dve.tensor_scalar(soft, soft, -LRU_C, None, ALU.mult))
                one_step(dve.memset(total[:, :], 0.0))

            dve.memset(eps, EPS).then_inc(eps_ready, 1)
            one_step(dve.memset(total[:, :], 0.0))
            dve.wait_ge(x_squared, 1)
            dve.tensor_reduce(stats[:, 0:META], meta_squares.rearrange("p j m -> p m j"), mybir.AxisListType.X, ALU.add)\
                .then_inc(x_summed, 1)
            for j in range(CT):
                dve.wait_ge(x_squared, j + 2)
                dve.wait_ge(x_summed, j + 1)
                dve.tensor_tensor(total[:, :], total[:, :], squares[:, j % 3, :], ALU.add).then_inc(x_summed, 1)
            dve.wait_ge(params_loaded, 16)
            dve.wait_ge(x_rms, 1)
            one_step(dve.reciprocal(psum[:, 6, 0:META], psum[:, 6, 0:META]))
            one_step(dve.tensor_tensor(meta_x, meta_x, psum[:, 6:7, 0:META].broadcast_to([P, CT, META]), ALU.mult))
            dve.tensor_tensor(meta_x, meta_x, params[:, :, NORM_G:NORM_G + 1].broadcast_to([P, CT, META]), ALU.mult)\
                .then_inc(x_normed, 1)
            one_step(dve.reciprocal(psum[:, 7, :], psum[:, 7, :]))
            dve.wait_ge(norm_hi, 1)
            dve.tensor_tensor(x_lo[:, :, 0:META], meta_x, x_hi[:, :, 0:META].bitcast(F32), ALU.subtract)\
                .then_inc(norm_lo, 1)

            branch_body(0, first=True)
            start = steps.total()
            with dve.Fori(1, PAIRS) as i:
                steps.at(plus(i * PER_BRANCH_BODY, start - PER_BRANCH_BODY))
                branch_body(i)
                assert steps.n == PER_BRANCH_BODY, steps.n
            steps.at(start + (PAIRS - 1) * PER_BRANCH_BODY)
            a_body(0, conv=True)
            a_body(1)
            dve.wait_ge(mean_ready, 1)
            one_step(dve.memset(total[:, :], 0.0))
            for n in range(4):
                dve.wait_ge(conv_b_loaded[n], 16)
            with dve.Fori(2, QUADS) as q:
                a_body(q, moments=True)
            b_body(0, first=True)
            start = steps.total()
            with dve.Fori(1, QUADS) as q:
                steps.at(plus(q * PER_B_BODY, start - PER_B_BODY))
                b_body(q)
                assert steps.n == PER_B_BODY, steps.n
            steps.at(start + (QUADS - 1) * PER_B_BODY)
            for q in range(CT // 8):
                for p in range(BODY):
                    cut_lo(B_B + q, p)
                    if p % 4 == 1 and (q, p) != (0, 1):
                        n = 4 * q + p // 4 - 1
                        merge(n // 4, n % 4)
            for n in range(D // 512):
                for p in range(8):
                    cut_lo(B_O + n // 2, 8 * (n % 2) + p)
                    if p == 1 and n == 0:
                        merge(CT // 8 - 1, 3)
                    if p == 1 and n > 0:
                        add_residual(n - 1)
            add_residual(D // 512 - 1)
            for t in range(TT):
                dve.wait_ge(out_squared, 4 * (D // 512 - 1) + t + 1)
                dve.tensor_reduce(rms[:, t:t + 1], sum_sq[:, 4 * t:4 * t + 4], mybir.AxisListType.X, ALU.add)\
                    .then_inc(out_rms, 1)
            dve.wait_ge(g_loaded, 16)
            for t in range(TT):
                dve.wait_ge(out_rstd, t + 1)
                one_step(dve.reciprocal(rstd[:, t:t + 1], rms[:, t:t + 1]))
                dve.scalar_tensor_tensor(tokens[:, t, :], tokens[:, t, :], rstd[:, t:t + 1], wide[:, :], ALU.mult, ALU.mult)\
                    .then_inc(out_ready, 1)


def kernel(x, meta, norm_g, w_in, conv_a_w, conv_a_b, w_rg, b_rg, w_ig, b_ig, lru_lambda, conv_b_w, conv_b_b,
           ln_b_g, ln_b_b, w_proj_a, w_proj_b, w_out, final_g):
    import numpy as np
    import concourse.bacc as bacc
    from concourse.bass_utils import run_bass_kernel_spmd

    _, seq, d = x.shape

    def by_channels(rows):
        return rows.reshape(-1, d // P, P).transpose(2, 1, 0)

    parameters = np.concatenate([norm_g, conv_a_b, b_rg, b_ig, lru_lambda, conv_b_b, ln_b_g, ln_b_b,
                                 conv_a_w[0], conv_b_w[0], np.zeros((2, d), norm_g.dtype)])
    inputs = {"x": x, "x_channels": by_channels(x[0]), "meta_channels": by_channels(meta),
              "parameters": by_channels(parameters), "w_in": w_in, "w_rg": w_rg, "w_ig": w_ig,
              "w_proj_a": w_proj_a, "w_proj_b": w_proj_b, "w_out": w_out, "final_g": final_g}

    nc = bacc.Bacc("TRN2", target_bir_lowering=False, num_devices=1)
    arrays, args = {}, []
    for name, value in inputs.items():
        a = np.ascontiguousarray(value)
        arrays[f"in_{name}"] = a
        args.append(nc.dram_tensor(f"in_{name}", a.shape, mybir.dt.from_np(a.dtype), kind="ExternalInput").ap())
    args += [conv_a_w.shape[1], conv_b_w.shape[1]]
    for name in ("conv_b_spill", "gated_a_spill"):
        args.append(nc.dram_tensor(name, (d // P, P, seq), F32, kind="Internal").ap())
    args.append(nc.dram_tensor("out_0", x.shape, F32, kind="ExternalOutput").ap())
    hybrid_trunk(nc, *args)
    r = run_bass_kernel_spmd(nc, [arrays], core_ids=[0])
    return r.results[0]["out_0"]
```

```python
from contextlib import ExitStack

import concourse.bass as bass
from concourse import mybir

ALU = mybir.AluOpType
ACT = mybir.ActivationFunctionType
F32 = mybir.dt.float32
F32R = mybir.dt.float32r
ds = bass.ds

P = 128
EPS = 1e-6
LRU_C = 8.0
BODY = 16
RING = 2
NORM_G, CONV_A_B, B_R, B_I, LAMBDA, CONV_B_B, LN_G, LN_B = range(8)
CONV_A_W = 8
PER_BRANCH_BODY, PER_B_BODY = 80, 22
WARM_UP = 18
SERIES = 8


def plus(base, n):
    return base + n if n else base


def wait(engine, semaphore, value):
    if not (isinstance(value, int) and value <= 0):
        engine.wait_ge(semaphore, value)


class Steps:

    def __init__(self, engine, semaphore):
        self.engine, self.semaphore, self.base, self.n = engine, semaphore, 0, 0

    def __call__(self, instruction):
        instruction.then_inc(self.semaphore, 1)
        self.n += 1
        return plus(self.base, self.n)

    def done(self, value):
        self.engine.wait_ge(self.semaphore, value)

    def at(self, base):
        self.base, self.n = base, 0

    def total(self):
        assert isinstance(self.base, int)
        return self.base + self.n


def hybrid_trunk(nc, x, x_channels, meta_channels, parameters, w_in, w_rg, w_ig, w_proj_a, w_proj_b, w_out,
                 final_g, kernel_a, kernel_b, conv_spill, gated_a_spill, out):
    D = x.shape[2]
    SEQ = x.shape[1]
    META = meta_channels.shape[2]
    T = META + SEQ
    HALF = T // 2
    CT = D // P
    TT = SEQ // P
    KA, KB = kernel_a, kernel_b
    CONV_B_W = CONV_A_W + KA
    ROWS = CONV_B_W + KB
    DECAY, HALF_DECAY, COLS = ROWS, ROWS + 1, ROWS + 2
    PAIRS = CT // 2
    QUADS = CT // 4
    assert (CT, TT, w_in.shape[0]) == (16, 4, 1) and T % 4 == 0
    COL_XA, COL_SA, COL_VB, COL_GB, COL_SB, COL_MA, COL_MB = (n * D for n in range(7))

    w_in_v = w_in[0].rearrange("(k p) n -> p k n", p=P)
    w_pa_v = w_proj_a[0].rearrange("(k p) n -> p k n", p=P)
    w_pb_v = w_proj_b[0].rearrange("(k p) n -> p k n", p=P)
    w_out_v = w_out[0].rearrange("(k p) n -> p k n", p=P)
    x_v = x[0].rearrange("(t p) d -> t p d", p=P)
    out_v = out[0].rearrange("(t p) d -> t p d", p=P)

    ctx = ExitStack()
    with ctx:
        def sb(name, shape, dt=F32):
            return ctx.enter_context(nc.sbuf_tensor(name, shape, dt))

        def sem(name):
            return ctx.enter_context(nc.semaphore(name))

        x_hi, x_lo = sb("x_hi", [P, CT, T], F32R), sb("x_lo", [P, CT, T], F32R)
        y_hi, y_lo = sb("y_hi", [P, CT, SEQ], F32R), sb("y_lo", [P, CT, SEQ], F32R)
        raw = sb("raw", [P, RING, 1024])
        w_hi, w_lo = sb("w_hi", [P, RING, 1024], F32R), sb("w_lo", [P, RING, 1024], F32R)
        raw_v, w_hi_v, w_lo_v = (t[:, :, :].rearrange("p s (k n) -> p s k n", k=4) for t in (raw, w_hi, w_lo))
        region = sb("region", [P, CT * SEQ])
        tokens = region[:, :].rearrange("p (t d) -> p t d", t=TT)
        channels = region[:, :].rearrange("p (j s) -> p j s", j=CT)
        used = [0]

        def work(n, width):
            a = region[:, used[0]:used[0] + n * width].rearrange("p (n w) -> p n w", n=n)
            used[0] += n * width
            assert used[0] <= CT * SEQ
            return a

        xa_pad = work(2, 4 + T)
        rec = xa_pad[:, :, 4:]
        conv_a = work(2, T)
        inp = work(2, T)
        decay = work(2, T)
        sig_gb = work(2, T)
        yb_pad = work(2, KB - 1 + T)
        conv_b = work(2, SEQ)
        wide = sb("wide", [P, D])
        gate_raw = wide[:, 0:512].rearrange("p (g h j) -> p g h j", g=2, h=2)
        silu_sa = wide[:, 512:512 + 2 * SEQ].rearrange("p (t s) -> p t s", t=2)
        pairs = wide[:, :].rearrange("p (s t n) -> p s t n", s=2, t=2)
        meta_x, meta_squares = (wide[:, n * CT * META:(n + 1) * CT * META].rearrange("p (j m) -> p j m", j=CT)
                                for n in range(2))
        squares = wide[:, 512:].rearrange("p (n s) -> p n s", n=3)
        gate_hi, gate_lo = (sb(n, [P, 2, 2, P], F32R) for n in ("gate_hi", "gate_lo"))
        c_hi, c_lo = sb("c_hi", [P, HALF], F32R), sb("c_lo", [P, HALF], F32R)
        params = sb("params", [P, CT, COLS])
        lru_cols, conv_cols = sb("lru_cols", [P, 2, COLS]), sb("conv_cols", [P, 2, COLS])
        total = sb("total", [P, SEQ])
        average = sb("average", [P, P])
        stats = sb("stats", [P, 72])
        psum = ctx.enter_context(nc.psum_tensor("psum", [P, 8, 512], F32))

        sum_sq, rms, rstd = stats[:, 0:16], stats[:, 16:24], stats[:, 24:32]
        eps = stats[:, 32:33]

        params_loaded, meta_loaded = sem("params_loaded"), sem("meta_loaded")
        x_loaded = [sem(f"x_loaded{n}") for n in range(PAIRS)]
        x_reloaded = [sem(f"x_reloaded{t}") for t in range(TT)]
        average_ready, eps_ready = sem("average_ready"), sem("eps_ready")
        lambda_abs, lambda_exp = sem("lambda_abs"), sem("lambda_exp")
        meta_squared, meta_summed, meta_mean, meta_rms, meta_normed, meta_hi, meta_lo = (
            sem(f"meta_{n}") for n in ("squared", "summed", "mean", "rms", "normed", "hi", "lo"))
        raw_x_hi, raw_x_lo = sem("raw_x_hi"), sem("raw_x_lo")
        x_squared, x_summed, x_mean, x_rms = sem("x_squared"), sem("x_summed"), sem("x_mean"), sem("x_rms")
        x_normed, norm_hi, norm_lo, norm_lo_pool = sem("x_normed"), sem("norm_hi"), sem("norm_lo"), sem("norm_lo_pool")
        sa_scaled, decay_columns_ready = sem("sa_scaled"), sem("decay_columns_ready")
        raw_loaded = [sem(f"raw_loaded{s}") for s in range(RING)]
        hi_ready, lo_ready, multiplied = sem("hi_ready"), sem("lo_ready"), sem("multiplied")
        xa_copied, conv_a_done, c_hi_ready, c_lo_ready = (
            sem("xa_copied"), sem("conv_a_done"), sem("c_hi_ready"), sem("c_lo_ready"))
        gate_loaded, gate_hi_ready, gate_lo_ready = (
            sem("gate_loaded"), sem("gate_hi_ready"), sem("gate_lo_ready"))
        gates_multiplied, gates_read = sem("gates_multiplied"), sem("gates_read")
        sa_sigmoid, sa_silu, decay_ready, root_ready = (
            sem("sa_sigmoid"), sem("sa_silu"), sem("decay_ready"), sem("root_ready"))
        lru_out, gb_sigmoid, vb_gated = sem("lru_out"), sem("gb_sigmoid"), sem("vb_gated")
        conv_b_done, conv_b_spilled = sem("conv_b_done"), sem("conv_b_spilled")
        conv_b_loaded = [sem(f"conv_b_loaded{n}") for n in range(4)]
        summed, mean_ready, centred, squared = (
            sem("summed"), sem("mean_ready"), sem("centred"), sem("squared"))
        var_ready, std_ready = sem("var_ready"), sem("std_ready")
        ma_sigmoid, a_gated = sem("ma_sigmoid"), sem("a_gated")
        a_spilled = [sem(f"a_spilled{s}") for s in range(2)]
        a_loaded = [sem(f"a_loaded{s}") for s in range(2)]
        ln_affine, ln_sigmoid, sb_sigmoid, yb_ready, mb_sigmoid = (
            sem("ln_affine"), sem("ln_sigmoid"), sem("sb_sigmoid"), sem("yb_ready"), sem("mb_sigmoid"))
        merged_ready, g_loaded = sem("merged_ready"), sem("g_loaded")
        last_multiplied, gained = sem("last_multiplied"), sem("gained")
        residual_added, out_squared, out_summed, out_rms, out_rstd = (
            sem("residual_added"), sem("out_squared"), sem("out_summed"), sem("out_rms"), sem("out_rstd"))
        out_ready, out_stored = [sem(f"out_ready{h}") for h in range(2)], sem("out_stored")
        act_done, dve_done = sem("act_done"), sem("dve_done")

        NORM_TILES = {5: range(0, 3), 6: range(3, 5), 8: range(5, 8), 9: range(8, 12), 10: range(12, CT)}
        LO_BY_DVE = 3

        B_A, B_N, B_B, B_O = PAIRS, PAIRS + QUADS, PAIRS + 2 * QUADS, PAIRS + 2 * QUADS + CT // 8
        LAST = D // 512 - 1
        OUT_STREAM = [divmod(n - n // 4, 8) if n % 4 < 3 else (LAST, n // 4) for n in range(2 * BODY)]
        assert LAST == 3

        block = ctx.enter_context(nc.Block())

        @block.sync
        def _(sp):
            def body(b, sources, x_too=False):
                for p, source in enumerate(sources):
                    if x_too and p < 4:
                        for n in (2 * p, 2 * p + 1):
                            sp.dma_start(channels[:, 2 * n:2 * n + 2, :], x_channels[:, 2 * n:2 * n + 2, :])\
                                .then_inc(x_loaded[n], 16)
                    wait(sp, lo_ready, plus(b * BODY, p + 1 - RING))
                    width = source.shape[2]
                    to = raw[:, p % RING, :].rearrange("p (k n) -> p k n", n=width)
                    sp.dma_start(to, source).then_inc(raw_loaded[p % RING], 16)

            def columns(view, start):
                return [view[:, 4 * q:4 * q + 4, ds(start, 256)] for q in range(4)]

            def branch_body(i, x_too=False):
                body(i, [c for col in (COL_XA, COL_SA, COL_GB, COL_VB)
                         for c in columns(w_in_v, plus(i * 256, col))], x_too)

            sp.dma_start(meta_x, meta_channels).then_inc(meta_loaded, 16)
            sp.dma_start(params[:, :, :], parameters).then_inc(params_loaded, 16)
            branch_body(0, x_too=True)
            with sp.Fori(1, PAIRS) as i:
                branch_body(i)
            with sp.Fori(B_A, B_A + QUADS) as b:
                body(b, [c for s in range(2) for view, col in ((w_in_v, COL_MA), (w_pa_v, 0))
                         for c in columns(view, plus(b * 512, col + 256 * s - B_A * 512))])
            with sp.Fori(0, QUADS) as q:
                body(q + B_N, [c for s in range(2) for col in (COL_SB, COL_MB)
                               for c in columns(w_in_v, plus(q * 512, col + 256 * s))])
            with sp.Fori(0, CT // 8) as q:
                body(q + B_B, [c for s in range(4) for c in columns(w_pb_v, plus(q * 1024, 256 * s))])
            for q in range(2):
                body(B_O + q, [w_out_v[:, 2 * g:2 * g + 2, n * 512:(n + 1) * 512]
                               for n, g in OUT_STREAM[q * BODY:(q + 1) * BODY]])
            for t in range(TT):
                for h in range(2):
                    sp.wait_ge(out_ready[h], t + 1)
                    sp.dma_start(out_v[t][:, h * D // 2:(h + 1) * D // 2], tokens[:, t, h * D // 2:(h + 1) * D // 2])\
                        .then_inc(out_stored, 16)
            sp.wait_ge(out_stored, 16 * 2 * TT)

        @block.gpsimd
        def _(pool):
            pool.memset(average[:, :], 1.0 / D).then_inc(average_ready, 1)

            def load_gates(i):
                wait(pool, gate_lo_ready, i)
                for g, w in enumerate((w_rg, w_ig)):
                    pool.dma_start(gate_raw[:, g], w[0, ds(2 * i, 2)].rearrange("h p j -> p h j"))\
                        .then_inc(gate_loaded, 16)

            def spill_conv(i):
                pool.wait_ge(conv_b_done, 2 * i)
                pool.dma_start(conv_spill[ds(2 * i - 2, 2)].rearrange("t p s -> p t s"), conv_b)\
                    .then_inc(conv_b_spilled, 16)

            def spill_a(q):
                for s in range(2):
                    pool.wait_ge(a_gated, plus(4 * q, 2 * s + 2))
                    pool.dma_start(gated_a_spill[ds(plus(4 * q, 2 * s), 2)].rearrange("t p s -> p t s"),
                                   pairs[:, s]).then_inc(a_spilled[s], 16)

            for j in range(1, CT):
                pool.wait_ge(x_squared, j + 1)
                wait(pool, x_summed, j - 1)
                pool.tensor_tensor(total[:, :], total[:, :], squares[:, j % 3, :], ALU.add).then_inc(x_summed, 1)
            pool.wait_ge(meta_lo, 1)
            load_gates(0)
            for j in range(LO_BY_DVE, CT):
                pool.wait_ge(norm_hi, j + 1)
                pool.tensor_tensor(x_lo[:, j, META:T], channels[:, j, :], x_hi[:, j, META:T].bitcast(F32),
                                   ALU.subtract).then_inc(norm_lo_pool, 1)
            with pool.Fori(1, PAIRS) as i:
                load_gates(i)
                spill_conv(i)
            spill_conv(PAIRS)
            spill_a(0)
            pool.wait_ge(conv_b_spilled, 16 * PAIRS)
            pool.wait_ge(mean_ready, 1)
            for n in range(4):
                pool.dma_start(channels[:, 4 * n:4 * n + 4], conv_spill[4 * n:4 * n + 4].rearrange("t p s -> p t s"))\
                    .then_inc(conv_b_loaded[n], 16)
            with pool.Fori(1, QUADS) as q:
                spill_a(q)

            def load_a(q, s):
                wait(pool, merged_ready, plus(8 * q, 2 * s - 2))
                pool.dma_start(pairs[:, s % 2], gated_a_spill[ds(plus(8 * q, 2 * s), 2)].rearrange("t p s -> p t s"))\
                    .then_inc(a_loaded[s % 2], 16)

            for s in range(2):
                pool.wait_ge(a_spilled[s], 16 * PAIRS // 2)
            pool.wait_ge(yb_ready, CT)
            for s in range(4):
                load_a(0, s)
            with pool.Fori(1, CT // 8) as q:
                for s in range(4):
                    load_a(q, s)
            pool.wait_ge(merged_ready, CT)
            for t in range(TT):
                pool.wait_ge(multiplied, B_O * BODY + 2 * t + 1)
                pool.dma_start(tokens[:, t, :], x_v[t]).then_inc(x_reloaded[t], 16)
            pool.wait_ge(multiplied, B_O * BODY + 2 * TT + 1)
            gain_rows = final_g.rearrange("(a d) -> a d", a=1).broadcast_to([P, D])
            pool.dma_start(wide[:, :], gain_rows).then_inc(g_loaded, 16)

        @block.tensor
        def _(pe):
            def multiply(b, p, tiles, group, raw_x=False):
                n = plus(b * BODY, p)

                def passes(weights, parts):
                    for k in range(4):
                        if raw_x and weights is w_hi_v:
                            pe.wait_ge(raw_x_lo, 4 * group + k + 1)
                        for m in range(2):
                            for part in parts:
                                for bank, width, operand, t0 in tiles[m]:
                                    last = pe.matmul(
                                        psum[:, bank, 0:width], weights[:, p % RING, k, m * P:(m + 1) * P],
                                        operand[part][:, 4 * group + k, t0:t0 + width],
                                        start=group == 0 and k == 0 and weights is w_hi_v and part == 0,
                                        stop=group == 3 and k == 3 and weights is w_lo_v)
                    return last

                pe.wait_ge(hi_ready, plus(n, 1))
                passes(w_hi_v, (0, 1))
                pe.wait_ge(lo_ready, plus(n, 1))
                passes(w_lo_v, (0,)).then_inc(multiplied, 1)

            def all_tokens(banks):
                return [[(pair[h], HALF, (x_hi, x_lo), h * HALF) for h in range(2)] for pair in banks]

            def x_tokens(banks):
                return [[(bank, SEQ, (x_hi, x_lo), META)] for bank in banks]

            def y_tokens(banks):
                return [[(bank, SEQ, (y_hi, y_lo), 0)] for bank in banks]

            def gate_round(i, n):
                pe.wait_ge(c_hi_ready, plus(4 * i, n + 1))
                pe.wait_ge(c_lo_ready, plus(4 * i, n + 1))
                wait(pe, gates_read, plus(4 * i, n))
                for g in range(2):
                    for weights, part in ((gate_hi, c_hi), (gate_hi, c_lo), (gate_lo, c_hi)):
                        last = pe.matmul(psum[:, 6 + g, 0:HALF], weights[:, g, n // 2, :], part[:, :],
                                         start=weights is gate_hi and part is c_hi, stop=weights is gate_lo)
                last.then_inc(gates_multiplied, 1)

            def branch_body(i, first=False):
                if first:
                    pe.wait_ge(meta_lo, 1)
                wait(pe, gb_sigmoid, 2 * i)
                for g in range(4):
                    multiply(i, g, all_tokens(((0, 1), (2, 3))), g, raw_x=first)
                if first:
                    pe.wait_ge(x_summed, CT - 1)
                    pe.matmul(psum[:, 7, :], average[:, :], total[:, :], start=True, stop=True).then_inc(x_mean, 1)
                wait(pe, vb_gated, 2 * i)
                for g in range(4):
                    multiply(i, 4 + g, x_tokens((4, 5)), g)
                pe.wait_ge(gate_hi_ready, plus(i, 1))
                pe.wait_ge(gate_lo_ready, plus(i, 1))
                pe.wait_ge(xa_copied, plus(2 * i, 2))
                for g in range(4):
                    gate_round(i, g)
                    if first:
                        pe.wait_ge(norm_lo, min(4 * g + 4, LO_BY_DVE))
                        wait(pe, norm_lo_pool, 4 * g + 4 - LO_BY_DVE)
                    multiply(i, 8 + g, all_tokens(((0, 1), (2, 3))), g)
                pe.wait_ge(sa_silu, plus(2 * i, 2))
                pe.wait_ge(gates_read, plus(4 * i, 4))
                for g in range(4):
                    multiply(i, 12 + g, all_tokens(((4, 5), (6, 7))), g)

            def a_body(q, mean=False):
                for s in range(2):
                    wait(pe, ma_sigmoid, plus(4 * q, 2 * s))
                    for g in range(4):
                        multiply(plus(q, B_A), 8 * s + g, x_tokens((0, 1)), g)
                        if mean and s == 0 and g == 3:
                            pe.wait_ge(summed, CT)
                            pe.wait_ge(average_ready, 1)
                            pe.matmul(psum[:, 7, :], average[:, :], total[:, :], start=True, stop=True)\
                                .then_inc(mean_ready, 1)
                    if isinstance(q, int) and (q, s) == (0, 0):
                        pe.wait_ge(lru_out, CT)
                    wait(pe, a_gated, plus(4 * q, 2 * s))
                    for g in range(4):
                        multiply(plus(q, B_A), 8 * s + 4 + g, y_tokens((2, 3)), g)

            def b_body(q):
                for s in range(2):
                    wait(pe, yb_ready, plus(4 * q, 2 * s))
                    for g in range(4):
                        multiply(plus(q, B_N), 8 * s + g, x_tokens((0, 1)), g)
                    if isinstance(q, int) and (q, s) == (0, 0):
                        pe.wait_ge(a_gated, CT)
                    wait(pe, mb_sigmoid, plus(2 * q, s))
                    for g in range(4):
                        multiply(plus(q, B_N), 8 * s + 4 + g, x_tokens((2, 3)), g)

            pe.wait_ge(average_ready, 1)
            for n in range(WARM_UP):
                if n == WARM_UP // 3:
                    pe.wait_ge(meta_summed, 1)
                    pe.matmul(psum[:, 6, 0:META], average[:, :], stats[:, 0:META], start=True, stop=True)\
                        .then_inc(meta_mean, 1)
                pe.matmul(psum[:, 7, 0:P], average[:, :], average[:, :], start=True, stop=True)
            branch_body(0, first=True)
            with pe.Fori(1, PAIRS) as i:
                branch_body(i)
            pe.wait_ge(gb_sigmoid, 2 * PAIRS)
            a_body(0)
            a_body(1, mean=True)
            with pe.Fori(2, QUADS) as q:
                a_body(q)
            pe.wait_ge(summed, 2 * CT)
            pe.matmul(psum[:, 6, :], average[:, :], total[:, :], start=True, stop=True).then_inc(var_ready, 1)
            b_body(0)
            with pe.Fori(1, QUADS) as q:
                b_body(q)

            for q in range(CT // 8):
                for s in range(4):
                    wait(pe, merged_ready, 8 * q + 2 * s - 6)
                    if (q, s) == (0, 1):
                        pe.wait_ge(mb_sigmoid, PAIRS)
                    for g in range(4):
                        if (q, s) == (0, 0):
                            pe.wait_ge(yb_ready, 4 * g + 4)
                        multiply(B_B + q, 4 * s + g, y_tokens((2 * s, 2 * s + 1)), g)

            for n in range(LAST):
                banks = 4 * (n % 2)
                wait(pe, out_squared, 4 * n - 4)
                for g in range(8):
                    if n == 0:
                        pe.wait_ge(merged_ready, max(2 * g + 2, CT - 4))
                    hi, lo = (w[:, g % RING, :].rearrange("p (k n) -> p k n", k=2) for w in (w_hi, w_lo))
                    for ready, weights, parts in ((hi_ready, hi, (x_hi, x_lo)), (lo_ready, lo, (x_hi,))):
                        pe.wait_ge(ready, B_O * BODY + OUT_STREAM.index((n, g)) + 1)
                        for t in range(TT):
                            for k in range(2):
                                for part in parts:
                                    last = pe.matmul(
                                        psum[:, banks + t, :], part[:, 2 * g + k, META + t * P:META + (t + 1) * P],
                                        weights[:, k, :],
                                        start=g == 0 and k == 0 and part is x_hi and weights is hi,
                                        stop=g == 7 and k == 1 and weights is lo)
                    last.then_inc(multiplied, 1)
            pe.wait_ge(out_squared, 4 * LAST - 4)
            pe.wait_ge(hi_ready, B_O * BODY + len(OUT_STREAM))
            pe.wait_ge(lo_ready, B_O * BODY + len(OUT_STREAM))
            for t in range(TT):
                for j in range(CT):
                    for part, weights in ((x_hi, y_hi), (x_lo, y_hi), (x_hi, y_lo)):
                        last = pe.matmul(psum[:, 4 * (LAST % 2) + t, :], part[:, j, META + t * P:META + (t + 1) * P],
                                         weights[:, j, :], start=j == 0 and part is x_hi and weights is y_hi,
                                         stop=j == CT - 1 and weights is y_lo)
                last.then_inc(last_multiplied, 1)

        @block.scalar
        def _(act):
            steps = Steps(act, act_done)

            def cut_hi(b, p):
                n = plus(b * BODY, p)
                act.wait_ge(raw_loaded[p % RING], plus(b * (16 * BODY // RING), 16 * (p // RING + 1)))
                wait(act, multiplied, plus(n, 1 - RING))
                act.activation(w_hi[:, p % RING, :], raw[:, p % RING, :], ACT.Copy).then_inc(hi_ready, 1)

            def group_done(b, chunks):
                act.wait_ge(multiplied, plus(b * BODY, chunks))

            def read_gates(i, n):
                t, tok = n // 2, slice((n % 2) * HALF, (n % 2 + 1) * HALF)
                act.wait_ge(gates_multiplied, plus(4 * i, n + 1))
                act.activation(rec[:, t, tok], psum[:, 6, 0:HALF], ACT.Sigmoid, bias=lru_cols[:, t, B_R:B_R + 1])
                act.activation(inp[:, t, tok], psum[:, 7, 0:HALF], ACT.Sigmoid, bias=lru_cols[:, t, B_I:B_I + 1])\
                    .then_inc(gates_read, 1)

            def cut_c_hi(i, n):
                t, tok = n // 2, slice((n % 2) * HALF, (n % 2 + 1) * HALF)
                act.wait_ge(conv_a_done, plus(2 * i, t + 1))
                wait(act, gates_multiplied, plus(4 * i, n))
                act.activation(c_hi[:, :], conv_a[:, t, tok], ACT.Copy).then_inc(c_hi_ready, 1)

            def raw_tiles(p):
                for j in range(4 * p, 4 * p + 4):
                    act.wait_ge(x_loaded[j // 2], 16)
                    act.activation(x_hi[:, j, META:T], channels[:, j, :], ACT.Copy,
                                   scale=params[:, j, NORM_G:NORM_G + 1]).then_inc(raw_x_hi, 1)
                    if j == 1:
                        act.wait_ge(meta_normed, 1)
                        act.activation(x_hi[:, :, 0:META], meta_x, ACT.Copy).then_inc(meta_hi, 1)
                cut_hi(0, p)
                for j in range(4 * p, 4 * p + 4):
                    wait(act, x_summed, j - 3)
                    act.activation(squares[:, j % 3, :] if j else total[:, :], channels[:, j, :], ACT.Square)\
                        .then_inc(x_squared, 1)

            def norm_tiles_hi(p):
                for j in NORM_TILES[p]:
                    act.wait_ge(x_normed, j + 1)
                    group_done(0, 5 + j // 4)
                    act.activation(x_hi[:, j, META:T], channels[:, j, :], ACT.Copy).then_inc(norm_hi, 1)

            def cut_gates_hi(i):
                act.wait_ge(gate_loaded, plus(32 * i, 32))
                wait(act, gates_multiplied, 4 * i)
                act.activation(gate_hi[:, :, :, :], gate_raw, ACT.Copy).then_inc(gate_hi_ready, 1)

            def sigmoid_sa(i, t):
                act.activation(silu_sa[:, t, :], psum[:, 4 + t, :], ACT.Sigmoid).then_inc(sa_sigmoid, 1)

            def first_body():
                for p in range(4):
                    raw_tiles(p)
                cut_hi(0, 4)
                act.wait_ge(x_mean, 1)
                act.activation(psum[:, 7, :], psum[:, 7, :], ACT.Sqrt, bias=eps).then_inc(x_rms, 1)
                cut_hi(0, 5)
                norm_tiles_hi(5)
                cut_hi(0, 6)
                norm_tiles_hi(6)
                cut_hi(0, 7)
                cut_gates_hi(0)
                cut_c_hi(0, 0)
                cut_hi(0, 8)
                norm_tiles_hi(8)
                cut_c_hi(0, 1)
                cut_hi(0, 9)
                act.wait_ge(norm_lo_pool, 7 - LO_BY_DVE)
                read_gates(0, 0)
                cut_c_hi(0, 2)
                norm_tiles_hi(9)
                cut_hi(0, 10)
                read_gates(0, 1)
                for t in range(2):
                    act.wait_ge(sa_scaled, t + 1)
                    sigmoid_sa(0, t)
                norm_tiles_hi(10)
                cut_c_hi(0, 3)
                cut_hi(0, 11)
                read_gates(0, 2)
                act.wait_ge(lambda_abs, 1)
                act.activation(stats[:, 0:CT], stats[:, 0:CT], ACT.Exp, scale=-1.0).then_inc(lambda_exp, 1)
                act.wait_ge(norm_lo_pool, CT - LO_BY_DVE)
                branch_end(0)

            def branch_body(i):
                for p in range(12):
                    cut_hi(i, p)
                    if p == 3:
                        cut_gates_hi(i)
                    if p == 5:
                        group_done(i, 4)
                        act.wait_ge(lru_out, 2 * i)
                        for t in range(2):
                            act.activation(xa_pad[:, t, 4:].rearrange("p (h n) -> p h n", h=2),
                                           psum[:, 2 * t:2 * t + 2, 0:HALF], ACT.Copy).then_inc(xa_copied, 1)
                    if p >= 8:
                        cut_c_hi(i, p - 8)
                    if p == 9:
                        group_done(i, 8)
                        for t in range(2):
                            sigmoid_sa(i, t)
                    if p >= 9:
                        read_gates(i, p - 9)
                branch_end(i)

            def branch_end(i):
                for p in range(12, BODY):
                    cut_hi(i, p)
                    if p == 12:
                        read_gates(i, 3)
                        act.wait_ge(gates_read, plus(4 * i, 4))
                        act.wait_ge(decay_columns_ready, 1)
                        for t in range(2):
                            act.activation(decay[:, t, :], rec[:, t, :], ACT.Exp,
                                           scale=lru_cols[:, t, DECAY:DECAY + 1]).then_inc(decay_ready, 1)
                        for t in range(2):
                            v = steps(act.activation(rec[:, t, :], rec[:, t, :], ACT.Tanh,
                                                     scale=lru_cols[:, t, HALF_DECAY:HALF_DECAY + 1]))
                    if p == 13:
                        steps.done(v)
                        for t in range(2):
                            act.activation(rec[:, t, :], rec[:, t, :], ACT.Sqrt).then_inc(root_ready, 1)
                    if p == 14:
                        group_done(i, 12)
                        for t in range(2):
                            act.activation(sig_gb[:, t, :].rearrange("p (h n) -> p h n", h=2),
                                           psum[:, 2 * t:2 * t + 2, 0:HALF], ACT.Sigmoid).then_inc(gb_sigmoid, 1)

            def a_body(q, squares=False):
                b = plus(q, B_A)
                for p in range(BODY):
                    cut_hi(b, p)
                    if p in (5, 13):
                        s = p // 8
                        group_done(b, 8 * s + 4)
                        wait(act, a_spilled[s], 16 * q)
                        if isinstance(q, int) and q == 0:
                            act.wait_ge(lru_out, CT)
                        for t in range(2):
                            act.activation(pairs[:, s, t, :], psum[:, t, :], ACT.Sigmoid).then_inc(ma_sigmoid, 1)
                    if squares and 2 <= p < 10:
                        u = p - 2
                        act.wait_ge(centred, plus(8 * q, u + 1 - 16))
                        act.wait_ge(summed, plus(8 * q, u - 1))
                        act.activation(psum[:, 4 + u % 2, :],
                                       channels[:, ds(plus(8 * q, u - 16), 1), :].rearrange("p a s -> p (a s)"),
                                       ACT.Square).then_inc(squared, 1)

            def read_mb(j):
                act.wait_ge(yb_ready, plus(2 * j, 2))
                act.activation(channels[:, ds(2 * j, 2), :], psum[:, 2:4, :], ACT.Sigmoid).then_inc(mb_sigmoid, 1)

            def b_body(q, first=False):
                b = plus(q, B_N)
                for p in range(BODY):
                    cut_hi(b, p)
                    if first and p == 0:
                        act.wait_ge(var_ready, 1)
                        act.activation(psum[:, 6, :], psum[:, 6, :], ACT.Sqrt, bias=eps).then_inc(std_ready, 1)
                    if p in (1, 9) and not (first and p == 1):
                        group_done(b, p - 1)
                        read_mb(plus(2 * q, p // 8 - 1))
                    if p in (2, 3, 10, 11):
                        s, t = p // 8, p % 2
                        j = plus(4 * q, 2 * s + t)
                        act.wait_ge(ln_affine, plus(j, 1))
                        act.activation(psum[:, 4 + t, :], channels[:, ds(j, 1), :].rearrange("p a s -> p (a s)"),
                                       ACT.Sigmoid).then_inc(ln_sigmoid, 1)
                    if p in (5, 13):
                        s = p // 8
                        group_done(b, 8 * s + 4)
                        if first and s == 0:
                            for n in range(2):
                                act.wait_ge(a_spilled[n], 16 * QUADS)
                        wait(act, yb_ready, plus(4 * q, 2 * s))
                        for t in range(2):
                            act.activation(pairs[:, 0, t, :], psum[:, t, :], ACT.Sigmoid).then_inc(sb_sigmoid, 1)

            act.wait_ge(eps_ready, 1)
            act.activation(stats[:, 33:34], eps, ACT.Sqrt)
            act.wait_ge(meta_loaded, 16)
            act.activation(meta_squares, meta_x, ACT.Square).then_inc(meta_squared, 1)
            act.wait_ge(meta_mean, 1)
            act.activation(psum[:, 6, 0:META], psum[:, 6, 0:META], ACT.Sqrt, bias=eps).then_inc(meta_rms, 1)
            act.wait_ge(params_loaded, 16)
            first_body()
            with act.Fori(1, PAIRS) as i:
                steps.at(2 * i)
                branch_body(i)
            a_body(0)
            a_body(1)
            with act.Fori(2, QUADS) as q:
                a_body(q, squares=True)
            b_body(0, first=True)
            with act.Fori(1, QUADS) as q:
                b_body(q)
            for p in range(2):
                cut_hi(B_B, p)
            group_done(B_B, 0)
            read_mb(PAIRS - 1)
            for p in range(2, BODY):
                cut_hi(B_B, p)
            for p in range(BODY):
                cut_hi(B_B + 1, p)

            def square_rows(n, t):
                act.wait_ge(residual_added, 4 * n + t + 1)
                act.activation(psum[:, 4 * (n % 2) + t, :], tokens[:, t, n * 512:(n + 1) * 512], ACT.Square,
                               accum_out=sum_sq[:, 4 * t + n:4 * t + n + 1]).then_inc(out_squared, 1)

            for i, (n, g) in enumerate(OUT_STREAM):
                act.wait_ge(raw_loaded[i % RING], 16 * ((B_O * BODY + i) // RING + 1))
                if n == LAST:
                    group_done(B_O, 0)
                    to = y_hi[:, 2 * g:2 * g + 2, :]
                else:
                    group_done(B_O, 8 * n + g + 1 - RING)
                    to = w_hi[:, g % RING, :].rearrange("p (k n) -> p k n", k=2)
                act.activation(to, raw[:, i % RING, :].rearrange("p (k n) -> p k n", k=2), ACT.Copy)\
                    .then_inc(hi_ready, 1)
                if n in (1, 2) and g == 3:
                    for t in range(TT):
                        square_rows(n - 1, t)
            for t in range(TT):
                square_rows(LAST - 1, t)
            for t in range(TT):
                square_rows(LAST, t)
                act.wait_ge(out_summed, t + 1)
                act.activation(rms[:, t:t + 1], rms[:, t:t + 1], ACT.Sqrt, scale=1.0 / D, bias=eps).then_inc(out_rms, 1)
                act.wait_ge(out_rstd, t + 1)
                act.wait_ge(gained, TT * LAST)
                act.activation(tokens[:, t, 0:D // 2], tokens[:, t, 0:D // 2], ACT.Copy, scale=rstd[:, t:t + 1])\
                    .then_inc(out_ready[0], 1)

        @block.vector
        def _(dve):
            steps = Steps(dve, dve_done)

            def cut_lo(b, p):
                dve.wait_ge(hi_ready, plus(b * BODY, p + 1))
                dve.tensor_tensor(w_lo[:, p % RING, :], raw[:, p % RING, :], w_hi[:, p % RING, :].bitcast(F32),
                                  ALU.subtract).then_inc(lo_ready, 1)

            def group_done(b, chunks):
                dve.wait_ge(multiplied, plus(b * BODY, chunks))

            def cut(values, done, hi, lo, j, tokens_of, ready):
                parts = [[part[:, ds(plus(j, t), 1), tokens_of].rearrange("p a s -> p (a s)") for t in range(2)]
                         for part in (hi, lo)]
                for t in range(2):
                    steps.done(done[t])
                    done[t] = steps(dve.tensor_copy(parts[0][t], values[t]))
                for t in range(2):
                    steps.done(done[t])
                    dve.tensor_tensor(parts[1][t], values[t], parts[0][t].bitcast(F32), ALU.subtract).then_inc(ready, 1)

            TAPS = [0, 3, 3, 3, 3, 1, 1, 3, 2, 3, 2, 3, 3, 1, 0, 0]
            assert sum(TAPS) == KB

            def conv_b_taps(i, p, before):
                for k in range(sum(TAPS[:p]), sum(TAPS[:p + 1])):
                    for t in range(2):
                        moved = yb_pad[:, t, META + k:META + k + SEQ]
                        w = conv_cols[:, t, CONV_B_W + k:CONV_B_W + k + 1]
                        if k == 0:
                            wait(dve, conv_b_spilled, 16 * (i - 1))
                            dve.wait_ge(vb_gated, plus(2 * i, t - 1))
                            ins = dve.tensor_scalar(conv_b[:, t, :], moved, w, conv_cols[:, t, CONV_B_B:CONV_B_B + 1],
                                                    ALU.mult, ALU.add)
                        else:
                            steps.done(before[t])
                            ins = dve.scalar_tensor_tensor(conv_b[:, t, :], moved, w, conv_b[:, t, :],
                                                           ALU.mult, ALU.add)
                        if k == KB - 1:
                            ins.then_inc(conv_b_done, 1)
                        else:
                            before[t] = steps(ins)

            def add_total(i):
                for t in range(2):
                    dve.wait_ge(conv_b_done, plus(2 * i, t - 1))
                    wait(dve, summed, plus(2 * i, t - 2))
                    dve.tensor_tensor(total[:, :], total[:, :], conv_b[:, t, :], ALU.add).then_inc(summed, 1)

            def conv_a_taps(i, taps, tiles, before):
                for k in taps:
                    for t in tiles:
                        moved = xa_pad[:, t, 4 - (KA - 1) + k:4 - (KA - 1) + k + T]
                        w = lru_cols[:, t, CONV_A_W + k:CONV_A_W + k + 1]
                        if k == 0:
                            dve.wait_ge(xa_copied, plus(2 * i, t + 1))
                            before[t] = steps(dve.tensor_scalar(
                                conv_a[:, t, :], moved, w, lru_cols[:, t, CONV_A_B:CONV_A_B + 1], ALU.mult, ALU.add))
                        else:
                            steps.done(before[t])
                            ins = dve.scalar_tensor_tensor(conv_a[:, t, :], moved, w, conv_a[:, t, :],
                                                           ALU.mult, ALU.add)
                            if k == KA - 1:
                                ins.then_inc(conv_a_done, 1)
                            else:
                                before[t] = steps(ins)

            def cut_gates_lo(i):
                dve.wait_ge(gate_hi_ready, plus(i, 1))
                dve.tensor_tensor(gate_lo[:, :, :, :], gate_raw, gate_hi[:, :, :, :].bitcast(F32), ALU.subtract)\
                    .then_inc(gate_lo_ready, 1)

            def cut_c_lo(i, n):
                t, tok = n // 2, slice((n % 2) * HALF, (n % 2 + 1) * HALF)
                dve.wait_ge(c_hi_ready, plus(4 * i, n + 1))
                dve.tensor_tensor(c_lo[:, :], conv_a[:, t, tok], c_hi[:, :].bitcast(F32), ALU.subtract)\
                    .then_inc(c_lo_ready, 1)

            def silu(i):
                for t in range(2):
                    dve.wait_ge(sa_sigmoid, plus(2 * i, t + 1))
                    dve.tensor_tensor(silu_sa[:, t, :], silu_sa[:, t, :], psum[:, 4 + t, :], ALU.mult)\
                        .then_inc(sa_silu, 1)

            def first_body():
                conv = [None, None]
                for p in range(4):
                    for j in range(4 * p, 4 * p + 4):
                        dve.wait_ge(raw_x_hi, j + 1)
                        dve.scalar_tensor_tensor(
                            x_lo[:, j, META:T], channels[:, j, :], params[:, j, NORM_G:NORM_G + 1],
                            x_hi[:, j, META:T].bitcast(F32), ALU.mult, ALU.subtract).then_inc(raw_x_lo, 1)
                    cut_lo(0, p)
                cut_lo(0, 4)
                one_step(dve.tensor_copy(lru_cols[:, :, 0:ROWS], params[:, 0:2, 0:ROWS]))
                dve.wait_ge(x_rms, 1)
                one_step(dve.reciprocal(total[:, :], psum[:, 7, :]))
                cut_lo(0, 5)
                norm_tiles(5)
                cut_lo(0, 6)
                norm_tiles(6)
                unscaled_xa()
                cut_lo(0, 7)
                dve.wait_ge(norm_lo_pool, 1)
                conv_a_taps(0, range(KA), (0,), conv)
                cut_gates_lo(0)
                cut_c_lo(0, 0)
                norm_tiles(8)
                cut_lo(0, 8)
                cut_c_lo(0, 1)
                dve.wait_ge(norm_lo_pool, 2)
                conv_a_taps(0, range(KA), (1,), conv)
                cut_lo(0, 9)
                norm_tiles(9)
                group_done(0, 8)
                for t in range(2):
                    dve.tensor_tensor(psum[:, 4 + t, :], psum[:, 4 + t, :], total[:, :], ALU.mult)\
                        .then_inc(sa_scaled, 1)
                cut_c_lo(0, 2)
                cut_lo(0, 10)
                norm_tiles(10)
                cut_c_lo(0, 3)
                silu(0)
                cut_lo(0, 11)
                absolute_lambda()
                dve.wait_ge(norm_lo_pool, CT - LO_BY_DVE)
                steps(dve.memset(yb_pad[:, :, 0:KB - 1], 0.0))
                one_step(dve.memset(total[:, :], 0.0))
                decay_columns()
                dve.tensor_copy(lru_cols[:, :, DECAY:COLS], params[:, 0:2, DECAY:COLS]).then_inc(decay_columns_ready, 1)
                branch_end(0, None)

            def branch_body(i):
                taps, conv = [None, None], [None, None]
                for p in range(12):
                    cut_lo(i, p)
                    if p == 0:
                        one_step(dve.tensor_copy(conv_cols[:, :, :], lru_cols[:, :, :]))
                        dve.wait_ge(root_ready, 2 * i)
                        one_step(dve.tensor_copy(lru_cols[:, :, :], params[:, ds(2 * i, 2), :]))
                    if p == 4:
                        cut_gates_lo(i)
                    if p in (5, 6):
                        conv_a_taps(i, range(2 * (p - 5), 2 * (p - 5) + 2), range(2), conv)
                    if p >= 8:
                        cut_c_lo(i, p - 8)
                    if p == 10:
                        silu(i)
                    conv_b_taps(i, p, taps)
                branch_end(i, taps)

            def branch_end(i, taps):
                for p in range(12, BODY):
                    cut_lo(i, p)
                    if p == 13:
                        dve.wait_ge(gates_read, plus(4 * i, 4))
                        gated = [steps(dve.tensor_tensor(inp[:, t, :], inp[:, t, :], conv_a[:, t, :], ALU.mult))
                                 for t in range(2)]
                    if p == 14:
                        factor = []
                        for t in range(2):
                            dve.wait_ge(root_ready, plus(2 * i, t + 1))
                            steps.done(gated[t])
                            factor.append(steps(dve.scalar_tensor_tensor(
                                conv_a[:, t, :], decay[:, t, :], 1.0, rec[:, t, :], ALU.add, ALU.mult)))
                        for t in range(2):
                            steps.done(factor[t])
                            factor[t] = steps(dve.tensor_tensor(inp[:, t, :], inp[:, t, :], conv_a[:, t, :], ALU.mult))
                    if p == 15:
                        state, gate = [], []
                        for t in range(2):
                            steps.done(factor[t])
                            state.append(steps(dve.tensor_tensor_scan(
                                rec[:, t, :], decay[:, t, :], inp[:, t, :], 0.0, ALU.mult, ALU.add)))
                        for t in range(2):
                            steps.done(state[t])
                            dve.wait_ge(sa_silu, plus(2 * i, t + 1))
                            gate.append(steps(dve.tensor_tensor(
                                silu_sa[:, t, :], rec[:, t, META:T], silu_sa[:, t, :], ALU.mult)))
                        cut([silu_sa[:, t, :] for t in range(2)], gate, y_hi, y_lo, 2 * i, slice(0, SEQ), lru_out)
                    if taps is not None:
                        conv_b_taps(i, p, taps)
                        if p == 14:
                            add_total(i)
                gate_vb(i)

            def gate_vb(i):
                group_done(i, 16)
                for t in range(2):
                    dve.wait_ge(gb_sigmoid, plus(2 * i, t + 1))
                    dve.tensor_tensor(yb_pad[:, t, KB - 1:].rearrange("p (h n) -> p h n", h=2),
                                      sig_gb[:, t, :].rearrange("p (h n) -> p h n", h=2),
                                      psum[:, 4 + 2 * t:6 + 2 * t, 0:HALF], ALU.mult).then_inc(vb_gated, 1)

            def channel(j):
                return channels[:, ds(j, 1), :].rearrange("p a s -> p (a s)")

            def a_body(q, conv=False, moments=False):
                b = plus(q, B_A)
                taps = [None, None]
                for p in range(BODY):
                    cut_lo(b, p)
                    if conv:
                        if p == 0:
                            c = steps(dve.tensor_copy(conv_cols[:, :, :], lru_cols[:, :, :]))
                            steps.done(c)
                        conv_b_taps(PAIRS, p, taps)
                        if p == 14:
                            add_total(PAIRS)
                    if p == 9:
                        gate_pa(q, b, 0)
                    if moments and 1 <= p < 9:
                        u = p - 1
                        j = plus(8 * q, u - 16)
                        dve.tensor_tensor(channel(j), channel(j), psum[:, 7, :], ALU.subtract).then_inc(centred, 1)
                    if moments and 3 <= p < 11:
                        u = p - 3
                        dve.wait_ge(squared, plus(8 * q, u + 1 - 16))
                        dve.wait_ge(summed, plus(8 * q, u))
                        dve.tensor_tensor(total[:, :], total[:, :], psum[:, 4 + u % 2, :], ALU.add).then_inc(summed, 1)
                gate_pa(q, b, 1)

            def gate_pa(q, b, s):
                group_done(b, 8 * s + 8)
                for t in range(2):
                    dve.wait_ge(ma_sigmoid, plus(4 * q, 2 * s + t + 1))
                    dve.tensor_tensor(pairs[:, s, t, :], pairs[:, s, t, :], psum[:, 2 + t, :], ALU.mult)\
                        .then_inc(a_gated, 1)

            def b_body(q, first=False):
                b = plus(q, B_N)
                for p in range(BODY):
                    cut_lo(b, p)
                    if first and p == 1:
                        dve.wait_ge(std_ready, 1)
                        one_step(dve.reciprocal(psum[:, 7, :], psum[:, 6, :]))
                    s, t = p // 8, p % 2
                    if p in (0, 8):
                        c = steps(dve.tensor_copy(lru_cols[:, :, :], params[:, ds(plus(4 * q, 2 * s), 2), :]))
                        steps.done(c)
                    if p in (1, 9):
                        scaled = []
                        for t in range(2):
                            c = channel(plus(4 * q, 2 * s + t))
                            scaled.append(steps(dve.tensor_tensor(c, c, psum[:, 7, :], ALU.mult)))
                        for t in range(2):
                            steps.done(scaled[t])
                            c = channel(plus(4 * q, 2 * s + t))
                            dve.tensor_scalar(c, c, lru_cols[:, t, LN_G:LN_G + 1], lru_cols[:, t, LN_B:LN_B + 1],
                                              ALU.mult, ALU.add).then_inc(ln_affine, 1)
                    if p in (4, 12):
                        silu = []
                        for t in range(2):
                            j = plus(4 * q, 2 * s + t)
                            dve.wait_ge(ln_sigmoid, plus(j, 1))
                            silu.append(steps(dve.tensor_tensor(channel(j), channel(j), psum[:, 4 + t, :], ALU.mult)))
                    if p in (6, 14):
                        v = []
                        for t in range(2):
                            dve.wait_ge(sb_sigmoid, plus(4 * q, 2 * s + t + 1))
                            v.append(steps(dve.tensor_tensor(pairs[:, 0, t, :], pairs[:, 0, t, :], psum[:, t, :],
                                                             ALU.mult)))
                        for t in range(2):
                            j = plus(4 * q, 2 * s + t)
                            steps.done(v[t])
                            v[t] = steps(dve.tensor_tensor(pairs[:, 0, t, :], pairs[:, 0, t, :], channel(j), ALU.mult))
                        cut([pairs[:, 0, t, :] for t in range(2)], v, y_hi, y_lo, plus(4 * q, 2 * s), slice(0, SEQ),
                            yb_ready)

            def merge(q, s):
                group_done(plus(q, B_B), 4 * s + 4)
                dve.wait_ge(mb_sigmoid, plus(4 * q, s + 1))
                v = [steps(dve.tensor_tensor(channel(plus(8 * q, 2 * s + t)), channel(plus(8 * q, 2 * s + t)),
                                             psum[:, 2 * s + t, :], ALU.mult)) for t in range(2)]
                dve.wait_ge(a_loaded[s % 2], plus(32 * q, 16 * (s // 2 + 1)))
                for t in range(2):
                    j = plus(8 * q, 2 * s + t)
                    steps.done(v[t])
                    v[t] = steps(dve.tensor_tensor(channel(j), channel(j), pairs[:, s % 2, t, :], ALU.add))
                cut([channel(plus(8 * q, 2 * s + t)) for t in range(2)], v, x_hi, x_lo, plus(8 * q, 2 * s),
                    slice(META, T), merged_ready)

            def add_residual(n, t):
                rows = tokens[:, t, n * 512:(n + 1) * 512]
                dve.wait_ge(x_reloaded[t], 16)
                dve.tensor_tensor(rows, rows, psum[:, 4 * (n % 2) + t, :], ALU.add).then_inc(residual_added, 1)

            def apply_gain(n):
                dve.wait_ge(g_loaded, 16)
                for t in range(TT):
                    rows = tokens[:, t, n * 512:(n + 1) * 512]
                    dve.wait_ge(out_squared, 4 * n + t + 1)
                    dve.tensor_tensor(rows, rows, wide[:, n * 512:(n + 1) * 512], ALU.mult).then_inc(gained, 1)

            def one_step(ins):
                steps.done(steps(ins))

            def tile_lo(j):
                dve.wait_ge(norm_hi, j + 1)
                dve.tensor_tensor(x_lo[:, j, META:T], channels[:, j, :], x_hi[:, j, META:T].bitcast(F32),
                                  ALU.subtract).then_inc(norm_lo, 1)

            def norm_tiles(p):
                for j in NORM_TILES[p]:
                    dve.scalar_tensor_tensor(channels[:, j, :], channels[:, j, :], params[:, j, NORM_G:NORM_G + 1],
                                             total[:, :], ALU.mult, ALU.mult).then_inc(x_normed, 1)
                    if 1 <= j <= LO_BY_DVE:
                        tile_lo(j - 1)

            def unscaled_xa():
                group_done(0, 4)
                dve.wait_ge(norm_lo, LO_BY_DVE)
                steps(dve.memset(xa_pad[:, :, 0:4], 0.0))
                for t in range(2):
                    steps(dve.tensor_copy(xa_pad[:, t, 4:4 + META], psum[:, 2 * t, 0:META]))
                    steps(dve.tensor_tensor(xa_pad[:, t, 4 + META:4 + HALF], psum[:, 2 * t, META:HALF],
                                            total[:, 0:HALF - META], ALU.mult))
                    dve.tensor_tensor(xa_pad[:, t, 4 + HALF:], psum[:, 2 * t + 1, 0:HALF], total[:, HALF - META:],
                                      ALU.mult).then_inc(xa_copied, 1)
                steps.done(steps.total())

            lam = params[:, :, LAMBDA:LAMBDA + 1].rearrange("p j c -> p (j c)")
            soft = params[:, :, DECAY:DECAY + 1].rearrange("p j c -> p (j c)")
            half_soft = params[:, :, HALF_DECAY:HALF_DECAY + 1].rearrange("p j c -> p (j c)")
            z, s, s2, series = (stats[:, n:n + CT] for n in (0, CT, 40, 40 + CT))

            def absolute_lambda():
                one_step(dve.tensor_scalar(s, lam, -1.0, None, ALU.mult))
                dve.tensor_tensor(z, lam, s, ALU.max).then_inc(lambda_abs, 1)
                one_step(dve.tensor_scalar(soft, s, 0.0, None, ALU.max))

            def decay_columns():
                dve.wait_ge(lambda_exp, 1)
                one_step(dve.tensor_scalar(s, z, 2.0, None, ALU.add))
                one_step(dve.reciprocal(s, s))
                one_step(dve.tensor_tensor(s, s, z, ALU.mult))
                one_step(dve.tensor_tensor(s2, s, s, ALU.mult))
                one_step(dve.tensor_scalar(series, s2, 1.0 / (2 * SERIES - 1), None, ALU.mult))
                for n in range(SERIES - 2, 0, -1):
                    one_step(dve.scalar_tensor_tensor(series, series, 1.0 / (2 * n + 1), s2, ALU.add, ALU.mult))
                one_step(dve.scalar_tensor_tensor(series, series, 1.0, s, ALU.add, ALU.mult))
                one_step(dve.scalar_tensor_tensor(soft, series, 2.0, soft, ALU.mult, ALU.add))
                one_step(dve.tensor_scalar(half_soft, soft, LRU_C / 2, None, ALU.mult))
                one_step(dve.tensor_scalar(soft, soft, -LRU_C, None, ALU.mult))

            dve.memset(eps, EPS).then_inc(eps_ready, 1)
            dve.wait_ge(meta_squared, 1)
            dve.tensor_reduce(stats[:, 0:META], meta_squares.rearrange("p j m -> p m j"), mybir.AxisListType.X,
                              ALU.add).then_inc(meta_summed, 1)
            dve.wait_ge(params_loaded, 16)
            dve.wait_ge(meta_rms, 1)
            one_step(dve.reciprocal(psum[:, 6, 0:META], psum[:, 6, 0:META]))
            one_step(dve.tensor_tensor(meta_x, meta_x, psum[:, 6:7, 0:META].broadcast_to([P, CT, META]), ALU.mult))
            dve.tensor_tensor(meta_x, meta_x, params[:, :, NORM_G:NORM_G + 1].broadcast_to([P, CT, META]), ALU.mult)\
                .then_inc(meta_normed, 1)
            dve.wait_ge(meta_hi, 1)
            dve.tensor_tensor(x_lo[:, :, 0:META], meta_x, x_hi[:, :, 0:META].bitcast(F32), ALU.subtract)\
                .then_inc(meta_lo, 1)

            first_body()
            start = steps.total()
            with dve.Fori(1, PAIRS) as i:
                steps.at(plus(i * PER_BRANCH_BODY, start - PER_BRANCH_BODY))
                branch_body(i)
                assert steps.n == PER_BRANCH_BODY, steps.n
            steps.at(start + (PAIRS - 1) * PER_BRANCH_BODY)
            a_body(0, conv=True)
            a_body(1)
            dve.wait_ge(mean_ready, 1)
            one_step(dve.memset(total[:, :], 0.0))
            for n in range(4):
                dve.wait_ge(conv_b_loaded[n], 16)
            with dve.Fori(2, QUADS) as q:
                a_body(q, moments=True)
            b_body(0, first=True)
            start = steps.total()
            with dve.Fori(1, QUADS) as q:
                steps.at(plus(q * PER_B_BODY, start - PER_B_BODY))
                b_body(q)
                assert steps.n == PER_B_BODY, steps.n
            steps.at(start + (QUADS - 1) * PER_B_BODY)
            for q in range(CT // 8):
                for p in range(BODY):
                    cut_lo(B_B + q, p)
                    if p % 4 == 1 and (q, p) != (0, 1):
                        n = 4 * q + p // 4 - 1
                        merge(n // 4, n % 4)
            for i, (n, g) in enumerate(OUT_STREAM):
                dve.wait_ge(hi_ready, B_O * BODY + i + 1)
                hi, lo = ((w[:, 2 * g:2 * g + 2, :] for w in (y_hi, y_lo)) if n == LAST else
                          (w[:, g % RING, :].rearrange("p (k n) -> p k n", k=2) for w in (w_hi, w_lo)))
                dve.tensor_tensor(lo, raw[:, i % RING, :].rearrange("p (k n) -> p k n", k=2), hi.bitcast(F32),
                                  ALU.subtract).then_inc(lo_ready, 1)
                if (n, g) == (0, 1):
                    merge(CT // 8 - 1, 3)
                if n in (1, 2) and g == 1:
                    group_done(B_O, 8 * n)
                    for t in range(TT):
                        add_residual(n - 1, t)
                if n in (1, 2) and g == 5:
                    apply_gain(n - 1)
            group_done(B_O, 8 * LAST)
            for t in range(TT):
                add_residual(LAST - 1, t)
            apply_gain(LAST - 1)
            for t in range(TT):
                dve.wait_ge(last_multiplied, t + 1)
                add_residual(LAST, t)
                dve.wait_ge(out_squared, TT * LAST + t + 1)
                dve.tensor_reduce(rms[:, t:t + 1], sum_sq[:, 4 * t:4 * t + 4], mybir.AxisListType.X, ALU.add)\
                    .then_inc(out_summed, 1)
                dve.wait_ge(out_rms, t + 1)
                dve.reciprocal(rstd[:, t:t + 1], rms[:, t:t + 1]).then_inc(out_rstd, 1)
                dve.wait_ge(out_rstd, t + 1)
                steps(dve.tensor_scalar(tokens[:, t, D // 2:LAST * 512], tokens[:, t, D // 2:LAST * 512],
                                        rstd[:, t:t + 1], None, ALU.mult))
                dve.scalar_tensor_tensor(tokens[:, t, LAST * 512:D], tokens[:, t, LAST * 512:D], rstd[:, t:t + 1],
                                         wide[:, LAST * 512:D], ALU.mult, ALU.mult).then_inc(out_ready[1], 1)


def kernel(x, meta, norm_g, w_in, conv_a_w, conv_a_b, w_rg, b_rg, w_ig, b_ig, lru_lambda, conv_b_w, conv_b_b,
           ln_b_g, ln_b_b, w_proj_a, w_proj_b, w_out, final_g):
    import numpy as np
    import concourse.bacc as bacc
    from concourse.bass_utils import run_bass_kernel_spmd

    _, seq, d = x.shape

    def by_channels(rows):
        return rows.reshape(-1, d // P, P).transpose(2, 1, 0)

    parameters = np.concatenate([norm_g, conv_a_b, b_rg, b_ig, lru_lambda, conv_b_b, ln_b_g, ln_b_b,
                                 conv_a_w[0], conv_b_w[0], np.zeros((2, d), norm_g.dtype)])
    inputs = {"x": x, "x_channels": by_channels(x[0]), "meta_channels": by_channels(meta),
              "parameters": by_channels(parameters), "w_in": w_in, "w_rg": w_rg, "w_ig": w_ig,
              "w_proj_a": w_proj_a, "w_proj_b": w_proj_b, "w_out": w_out, "final_g": final_g}

    nc = bacc.Bacc("TRN2", target_bir_lowering=False, num_devices=1)
    arrays, args = {}, []
    for name, value in inputs.items():
        a = np.ascontiguousarray(value)
        arrays[f"in_{name}"] = a
        args.append(nc.dram_tensor(f"in_{name}", a.shape, mybir.dt.from_np(a.dtype), kind="ExternalInput").ap())
    args += [conv_a_w.shape[1], conv_b_w.shape[1]]
    for name in ("conv_b_spill", "gated_a_spill"):
        args.append(nc.dram_tensor(name, (d // P, P, seq), F32, kind="Internal").ap())
    args.append(nc.dram_tensor("out_0", x.shape, F32, kind="ExternalOutput").ap())
    hybrid_trunk(nc, *args)
    r = run_bass_kernel_spmd(nc, [arrays], core_ids=[0])
    return r.results[0]["out_0"]
```
